# Optimizing a Trainium2 kernel written in Bass

```python
import jax, jax.numpy as jnp
from jax import lax
import numpy as np

D_MODEL = 2048
BATCH = 1
SEQ = 256
DEPTH = 2

N_A_LAYERS = max(1, DEPTH // 2)
N_B_LAYERS = DEPTH - N_A_LAYERS
D_SGU = D_MODEL
SGU_CHUNK = 128
SGU_GROUPS = 16
SGU_GROUP_DIM = D_SGU // SGU_GROUPS
HEAD_DIM = 128
N_HEADS = D_MODEL // HEAD_DIM
MOBA_BLOCK = 256
MOBA_TOPK = 3
Q_CHUNK = 8
D_FF = -(-8 * D_MODEL // (3 * 256)) * 256
EPS = 1e-6

kernel_name = "yoco_sgu_moba_hybrid"

def rms_norm(x, g):
    xf = x.astype(jnp.float32)
    y = xf * lax.rsqrt(jnp.mean(xf * xf, axis=-1, keepdims=True) + EPS)
    return (y * g.astype(jnp.float32)).astype(x.dtype)

def layer_norm(x, g, b):
    xf = x.astype(jnp.float32)
    mu = jnp.mean(xf, axis=-1, keepdims=True)
    var = jnp.mean(jnp.square(xf - mu), axis=-1, keepdims=True)
    y = (xf - mu) * lax.rsqrt(var + EPS)
    return (y * g.astype(jnp.float32) + b.astype(jnp.float32)).astype(x.dtype)

def swiglu_ffn(x, norm_g, w_gate, w_up, w_down):
    h = rms_norm(x, norm_g)
    return (jax.nn.silu(h @ w_gate) * (h @ w_up)) @ w_down

def chunked_sgu_mixer(x, norm_g, w_in, ln_g, ln_b, w_s, b_s, w_out):
    B, S, _ = x.shape
    n_chunks = S // SGU_CHUNK
    z = jax.nn.gelu(rms_norm(x, norm_g) @ w_in)
    u, v = jnp.split(z, 2, axis=-1)
    v = layer_norm(v, ln_g, ln_b)
    v = v.reshape(B, n_chunks, SGU_CHUNK, SGU_GROUPS, SGU_GROUP_DIM)
    causal = jnp.tril(jnp.ones((SGU_CHUNK, SGU_CHUNK), dtype=w_s.dtype))
    w = w_s * causal
    mixed = jnp.einsum('gts,bcsgd->bctgd', w, v) + b_s.T[None, None, :, :, None]
    gate = mixed.reshape(B, S, D_SGU)
    return (u * gate) @ w_out

def shared_kv(x, kv_norm, w_k, w_v, k_norm):
    B, S, _ = x.shape
    h = rms_norm(x, kv_norm)
    k = rms_norm((h @ w_k).reshape(B, S, N_HEADS, HEAD_DIM), k_norm).transpose(0, 2, 1, 3)
    v = (h @ w_v).reshape(B, S, N_HEADS, HEAD_DIM).transpose(0, 2, 1, 3)
    n_blocks = -(-S // MOBA_BLOCK)
    pad = n_blocks * MOBA_BLOCK - S
    k = jnp.pad(k, ((0, 0), (0, 0), (0, pad), (0, 0)))
    v = jnp.pad(v, ((0, 0), (0, 0), (0, pad), (0, 0)))
    k_blk = k.reshape(B, N_HEADS, n_blocks, MOBA_BLOCK, HEAD_DIM)
    v_blk = v.reshape(B, N_HEADS, n_blocks, MOBA_BLOCK, HEAD_DIM)
    k_mean = jnp.mean(k_blk.astype(jnp.float32), axis=3).astype(k_blk.dtype)
    return k_blk, v_blk, k_mean

def moba_attention(x, norm_g, w_q, q_norm, w_o, k_blk, v_blk, k_mean):
    B, S, _ = x.shape
    n_blocks = k_blk.shape[2]
    n_sel = min(MOBA_TOPK, n_blocks - 1)
    n_chunks = S // Q_CHUNK
    q = rms_norm((rms_norm(x, norm_g) @ w_q).reshape(B, S, N_HEADS, HEAD_DIM), q_norm)
    q = (q * (HEAD_DIM ** -0.5)).transpose(0, 2, 1, 3)
    q_c = q.reshape(B, N_HEADS, n_chunks, Q_CHUNK, HEAD_DIM).transpose(2, 0, 1, 3, 4)
    xs = (jnp.arange(n_chunks, dtype=jnp.int32), q_c)
    if n_sel > 0:
        q_block = jnp.arange(S) // MOBA_BLOCK
        gate = jnp.einsum('bhsd,bhnd->bhsn', q, k_mean).astype(jnp.float32)
        past = jnp.arange(n_blocks)[None, :] < q_block[:, None]
        gate = jnp.where(past, gate, -jnp.inf)
        top_val, top_idx = lax.top_k(gate, n_sel)
        valid = jnp.isfinite(top_val)
        to_chunks = lambda a: a.reshape(B, N_HEADS, n_chunks, Q_CHUNK, n_sel).transpose(2, 0, 1, 3, 4)
        xs = xs + (to_chunks(top_idx), to_chunks(valid))
    b_idx = jnp.arange(B)[:, None, None, None]
    h_idx = jnp.arange(N_HEADS)[None, :, None, None]

    def attend(args):
        c, qc = args[0], args[1]
        q_pos = c * Q_CHUNK + jnp.arange(Q_CHUNK)
        blk = (c * Q_CHUNK) // MOBA_BLOCK
        k_own = lax.dynamic_index_in_dim(k_blk, blk, axis=2, keepdims=False)
        v_own = lax.dynamic_index_in_dim(v_blk, blk, axis=2, keepdims=False)
        k_pos = blk * MOBA_BLOCK + jnp.arange(MOBA_BLOCK)
        s_own = jnp.einsum('bhqd,bhkd->bhqk', qc, k_own).astype(jnp.float32)
        s_own = jnp.where(k_pos[None, :] <= q_pos[:, None], s_own, -jnp.inf)
        if n_sel == 0:
            p = jax.nn.softmax(s_own, axis=-1).astype(qc.dtype)
            return jnp.einsum('bhqk,bhkd->bhqd', p, v_own)
        idx, ok = args[2], args[3]
        k_sel = k_blk[b_idx, h_idx, idx]
        v_sel = v_blk[b_idx, h_idx, idx]
        s_sel = jnp.einsum('bhqd,bhqnkd->bhqnk', qc, k_sel).astype(jnp.float32)
        s_sel = jnp.where(ok[..., None], s_sel, -jnp.inf)
        s_sel = s_sel.reshape(B, N_HEADS, Q_CHUNK, n_sel * MOBA_BLOCK)
        p = jax.nn.softmax(jnp.concatenate([s_own, s_sel], axis=-1), axis=-1).astype(qc.dtype)
        p_own = p[..., :MOBA_BLOCK]
        p_sel = p[..., MOBA_BLOCK:].reshape(B, N_HEADS, Q_CHUNK, n_sel, MOBA_BLOCK)
        return (jnp.einsum('bhqk,bhkd->bhqd', p_own, v_own)
                + jnp.einsum('bhqnk,bhqnkd->bhqd', p_sel, v_sel))

    out = lax.map(attend, xs)
    out = out.transpose(1, 0, 3, 2, 4).reshape(B, S, D_MODEL)
    return out @ w_o

def setup_inputs(seed: int = 0) -> dict:
    key = jax.random.key(seed)
    ks = iter(jax.random.split(key, 32))
    f32 = jnp.float32
    nrm = lambda shape, scale: jax.random.normal(next(ks), shape, f32) * scale
    gain = lambda shape: 1.0 + 0.02 * jax.random.normal(next(ks), shape, f32)
    return {
        "x": jax.random.normal(next(ks), (BATCH, SEQ, D_MODEL), f32),
        "a_norm": gain((N_A_LAYERS, D_MODEL)),
        "a_w_in": nrm((N_A_LAYERS, D_MODEL, 2 * D_SGU), D_MODEL ** -0.5),
        "a_ln_g": gain((N_A_LAYERS, D_SGU)),
        "a_ln_b": nrm((N_A_LAYERS, D_SGU), 0.02),
        "a_w_s": nrm((N_A_LAYERS, SGU_GROUPS, SGU_CHUNK, SGU_CHUNK), SGU_CHUNK ** -0.5),
        "a_b_s": gain((N_A_LAYERS, SGU_GROUPS, SGU_CHUNK)),
        "a_w_out": nrm((N_A_LAYERS, D_SGU, D_MODEL), D_SGU ** -0.5),
        "kv_norm": gain((D_MODEL,)),
        "w_k": nrm((D_MODEL, D_MODEL), D_MODEL ** -0.5),
        "w_v": nrm((D_MODEL, D_MODEL), D_MODEL ** -0.5),
        "k_norm": gain((HEAD_DIM,)),
        "b_norm": gain((N_B_LAYERS, D_MODEL)),
        "b_w_q": nrm((N_B_LAYERS, D_MODEL, D_MODEL), D_MODEL ** -0.5),
        "b_q_norm": gain((N_B_LAYERS, HEAD_DIM)),
        "b_w_o": nrm((N_B_LAYERS, D_MODEL, D_MODEL), D_MODEL ** -0.5),
        "ffn_norm": gain((DEPTH, D_MODEL)),
        "ffn_w_gate": nrm((DEPTH, D_MODEL, D_FF), D_MODEL ** -0.5),
        "ffn_w_up": nrm((DEPTH, D_MODEL, D_FF), D_MODEL ** -0.5),
        "ffn_w_down": nrm((DEPTH, D_FF, D_MODEL), D_FF ** -0.5),
    }

def reference(x, a_norm, a_w_in, a_ln_g, a_ln_b, a_w_s, a_b_s, a_w_out,
              kv_norm, w_k, w_v, k_norm, b_norm, b_w_q, b_q_norm, b_w_o,
              ffn_norm, ffn_w_gate, ffn_w_up, ffn_w_down):
    kv = None
    for layer in range(DEPTH):
        if layer < N_A_LAYERS:
            i = layer
            x = x + chunked_sgu_mixer(x, a_norm[i], a_w_in[i], a_ln_g[i], a_ln_b[i],
                                      a_w_s[i], a_b_s[i], a_w_out[i])
        else:
            if kv is None:
                kv = shared_kv(x, kv_norm, w_k, w_v, k_norm)
            i = layer - N_A_LAYERS
            x = x + moba_attention(x, b_norm[i], b_w_q[i], b_q_norm[i], b_w_o[i], *kv)
        x = x + swiglu_ffn(x, ffn_norm[layer], ffn_w_gate[layer], ffn_w_up[layer], ffn_w_down[layer])
    return x


_drawn_inputs = setup_inputs


def setup_inputs(seed=0):
    import zlib

    import numpy as np

    out = dict(_drawn_inputs(seed))
    spreads = {}
    factors = {'a_norm': 3.049,
     'a_ln_g': 7.11,
     'a_ln_b': 6.998,
     'a_b_s': 4.636,
     'kv_norm': 8.0,
     'k_norm': 8.0,
     'b_norm': 8.0,
     'b_q_norm': 8.0,
     'ffn_norm': 3.37}
    for name, (base, spread) in spreads.items():
        noise = np.random.default_rng([zlib.crc32(name.encode()), seed]).standard_normal(out[name].shape)
        drawn = base * np.exp(spread * noise) if base else spread * noise
        out[name] = __import__('jax').numpy.asarray(drawn.astype(out[name].dtype))
    for name, factor in factors.items():
        out[name] = (out[name] * factor).astype(out[name].dtype)
    return out
```

```python
from contextlib import ExitStack

import concourse.bass as bass
from concourse import mybir

F32 = mybir.dt.float32
F32R = mybir.dt.float32r
ACT = mybir.ActivationFunctionType
ALU = mybir.AluOpType
AX_X = mybir.AxisListType.X

P = 128
CH = 512
HG = 2
RAW = 4
RING = 4
EPS = 1e-6
NEG = -1e30


class Tally:

    def __init__(self, engine, sem):
        self.engine, self.sem = engine, sem
        self.base = self.n = self.per = 0
        self.i = None

    def inc(self, instruction):
        instruction.then_inc(self.sem, 1)
        self.n += 1
        return instruction

    def wait(self):
        count = self.base + self.n
        self.engine.wait_ge(self.sem, count if self.i is None else self.i * self.per + count)

    def enter(self, i, per, first=0):
        self.base, self.n = self.base + self.n - first * per, 0
        self.i, self.per = i, per

    def leave(self, end):
        assert self.n == self.per, (self.n, self.per)
        self.base, self.n, self.i = self.base + self.per * end, 0, None


def yoco_kernel(nc, x, a_norm, a_w_in, a_ln_g, a_ln_b, a_w_s, a_b_s, a_w_out, kv_norm, w_k, w_v, k_norm,
                b_norm, b_w_q, b_q_norm, b_w_o, ffn_norm, ffn_w_gate, ffn_w_up, ffn_w_down, out):
    _, S, D = x.shape
    F = ffn_w_gate.shape[2]
    G = a_w_s.shape[1]
    TT = S // P
    KB = D // P
    FB = F // P
    NC = D // CH
    NF = F // CH
    HPC = CH // P
    assert TT == 2 and KB == 16 and NC == 4 and G == KB and HPC == 4 and k_norm.shape[0] == P
    assert a_w_s.shape[2] == P and FB % 4 == 0 and (2 * FB // HG) % RING == 0

    PHASES = [("v", NC, KB), ("u", NC, KB), ("wout", NC, KB), ("gu0", 2 * NF, KB), ("down0", NC, FB),
              ("qkv", 3 * NC, KB), ("wo", NC, KB), ("gu1", 2 * NF, KB), ("down1", NC, FB)]
    hg_before, slot_before = {}, {}
    hg, slots = 0, [0] * RAW
    for name, units, kb in PHASES:
        hg_before[name], slot_before[name] = hg, list(slots)
        hg += units * kb // HG
        per_body = (1 if kb == KB else 2) * kb // (2 * HG)
        for g in range(units * kb // (2 * HG)):
            slots[g % per_body % RAW] += 1
    batches = {"x": 0, "gated": NC, "x1": 2 * NC, "h0": 3 * NC, "x2": 3 * NC + NF, "o": 4 * NC + NF,
               "x3": 5 * NC + NF, "h1": 6 * NC + NF, "out": 6 * NC + 2 * NF}

    w_in_v = a_w_in[0, :, D:2 * D].rearrange("(k p) n -> p k n", p=P)
    w_in_u = a_w_in[0, :, 0:D].rearrange("(k p) n -> p k n", p=P)
    w_out_k = a_w_out[0, :, :].rearrange("(k p) n -> p k n", p=P)
    w_gate_k = [ffn_w_gate[n, :, :].rearrange("(k p) n -> p k n", p=P) for n in range(2)]
    w_up_k = [ffn_w_up[n, :, :].rearrange("(k p) n -> p k n", p=P) for n in range(2)]
    w_down_k = [ffn_w_down[n, :, :].rearrange("(k p) n -> p k n", p=P) for n in range(2)]
    w_v_k = w_v.rearrange("(k p) n -> p k n", p=P)
    w_k_k = w_k.rearrange("(k p) n -> p k n", p=P)
    w_q_k = b_w_q[0, :, :].rearrange("(k p) n -> p k n", p=P)
    w_o_k = b_w_o[0, :, :].rearrange("(k p) n -> p k n", p=P)
    x_tiles = x[0, :, :].rearrange("(t p) n -> p t n", p=P)
    out_tiles = out[0, :, :].rearrange("(t p) n -> p t n", p=P)

    with ExitStack() as ctx:
        def sb(name, shape, dt, scope=ctx):
            return scope.enter_context(nc.sbuf_tensor(name, shape, dt))

        def sem(name):
            return ctx.enter_context(nc.semaphore(name))

        raw = sb("raw", [P, RAW, 2 * HG, CH], F32)
        w_hi = sb("w_hi", [P, RING, HG, CH], F32R)
        w_lo = sb("w_lo", [P, RING, HG, CH], F32R)
        a_hi = sb("a_hi", [P, KB, S], F32R)
        a_lo = sb("a_lo", [P, KB, S], F32R)
        res = sb("res", [P, TT, D], F32)
        stage = sb("stage", [P, TT, CH], F32)
        ident = sb("ident", [P, P], F32)
        junk_b = sb("junk_b", [P, CH], mybir.dt.bfloat16)
        gains = sb("gains", [P, 6 * KB], F32)
        head_gain = sb("head_gain", [P, 2], F32)
        sums = sb("sums", [P, 4, TT, NC], F32)
        rstd = sb("rstd", [P, 4, TT], F32)
        power = sb("power", [P, 8], F32)
        ln_stats = sb("ln_stats", [P, TT, NC, 6], F32)
        ln_mv = sb("ln_mv", [P, TT, 2], F32)
        ln_rstd = sb("ln_rstd", [P, TT], F32)
        head_ss = sb("head_ss", [P, 2, TT, HPC], F32)
        head_rs = sb("head_rs", [P, 2, TT, HPC], F32)
        neg_max = sb("neg_max", [P, TT], F32)
        row_sum = sb("row_sum", [P, TT], F32)
        row_inv = sb("row_inv", [P, TT], F32)
        A_NORM, KV_NORM, B_NORM, FFN0, FFN1, B_S = (n * KB for n in range(6))

        with ExitStack() as part:
            g_hi = sb("g_hi", [P, KB, S], F32R, part)
            g_lo = sb("g_lo", [P, KB, S], F32R, part)
            v_nat = sb("v_nat", [P, TT, D], F32, part)
            ln_gain = sb("ln_gain", [P, D], F32, part)
            ln_bias = sb("ln_bias", [P, D], F32, part)
            w_sT = sb("w_sT", [P, G, P], F32, part)
            u_nat = sb("u_nat", [P, TT, CH], F32, part)
        with ExitStack() as part:
            w_s_nat = sb("w_s_nat", [P, G, P], F32, part)
            junk_a = sb("junk_a", [P, D], F32, part)
            rows = sb("rows", [6 * KB, P], F32, part)
        with ExitStack() as part:
            h_hi = sb("h_hi", [P, FB, S], F32R, part)
            h_lo = sb("h_lo", [P, FB, S], F32R, part)
        with ExitStack() as part:
            o_hi = sb("o_hi", [P, KB, S], F32R, part)
            o_lo = sb("o_lo", [P, KB, S], F32R, part)
            val = sb("val", [P, TT, D], F32, part)
            k_nat = sb("k_nat", [P, TT, HPC, P], F32, part)
            q_nat = sb("q_nat", [P, TT, HPC, P], F32, part)
            kT = sb("kT", [P, HPC, S], F32, part)
            qT = sb("qT", [P, HPC, S], F32, part)
            sq_nat = sb("sq_nat", [P, TT, HPC, P], F32, part)
            mask = sb("mask", [P, 3, P], F32, part)
            score = sb("score", [P, 3, P], F32, part)
            prob = sb("prob", [P, 3, P], F32, part)
            probT = sb("probT", [P, 3, P], F32, part)

        acc = [[ctx.enter_context(nc.psum_tensor(f"acc{s}_{t}", [P, CH], F32)) for t in range(TT)] for s in range(3)]
        tr = [ctx.enter_context(nc.psum_tensor(f"tr{j}", [P, CH], F32)) for j in range(2)]

        raw_landed = [sem(f"raw_landed{s}") for s in range(RAW)]
        hi_split = sem("hi_split")
        lo_split = sem("lo_split")
        w_used = sem("w_used")
        staged = sem("staged")
        transposed = sem("transposed")
        lhs_hi = sem("lhs_hi")
        lhs_lo = sem("lhs_lo")
        res_saved = sem("res_saved")
        x_landed = [sem(f"x_landed{c}") for c in range(NC)]
        rows_landed, ws_landed, ln_landed = sem("rows_landed"), sem("ws_landed"), sem("ln_landed")
        hgain_landed = sem("hgain_landed")
        ident_ready, mask_ready, ws_masked = sem("ident_ready"), sem("mask_ready"), sem("ws_masked")
        rows_transposed, gains_ready = sem("rows_transposed"), sem("gains_ready")
        sums_ready = sem("sums_ready")
        ms_ready = sem("ms_ready")
        rstd_ready = sem("rstd_ready")
        wsT_done, wsT_ready = sem("wsT_done"), sem("wsT_ready")
        v_ready, mv_ready, ln_rstd_ready, ln_done = sem("v_ready"), sem("mv_ready"), sem("ln_rstd_ready"), sem("ln_done")
        u_ready, mixed = sem("u_ready"), sem("mixed")
        silu_ready = sem("silu_ready")
        val_ready = sem("val_ready")
        kq_raw, kq_squared, kq_ss, kq_rs = sem("kq_raw"), sem("kq_squared"), sem("kq_ss"), sem("kq_rs")
        kq_normed, kq_transposed, kq_ready = sem("kq_normed"), sem("kq_transposed"), sem("kq_ready")
        scored, maxed, exped = sem("scored"), sem("maxed"), sem("exped")
        probT_done, probT_ready, pv_done, head_out = sem("probT_done"), sem("probT_ready"), sem("pv_done"), sem("head_out")
        pool_step, act_step, dve_step = sem("pool_step"), sem("act_step"), sem("dve_step")
        stored = sem("stored")

        block = ctx.enter_context(nc.Block())

        @block.sync
        def _(sp):
            def load(slot, src, prev_hg):
                if prev_hg is not None:
                    sp.wait_ge(lo_split, prev_hg)
                sp.dma_start(raw[:, slot, :, :], src).then_inc(raw_landed[slot], 16)

            def load_unit(w, col, hg0, first=False, after_down=False):
                for j in range(KB // 4):
                    back = None if first else (2 if after_down and j < 2 else 6)
                    load(j, w[:, 4 * j:4 * j + 4, bass.ds(col, CH)],
                         None if back is None else hg0 + 2 * j - back)

            for c in range(NC):
                sp.dma_start(res[:, :, c * CH:(c + 1) * CH], x_tiles[:, :, c * CH:(c + 1) * CH])\
                    .then_inc(x_landed[c], 16)
            load_unit(w_in_v, 0, 0, first=True)
            with sp.Fori(1, NC) as i:
                load_unit(w_in_v, i * CH, i * 8)
            with sp.Fori(0, NC) as i:
                load_unit(w_in_u, i * CH, i * 8 + hg_before["u"])
            with sp.Fori(0, NC) as i:
                load_unit(w_out_k, i * CH, i * 8 + hg_before["wout"])

            def gate_up(layer):
                base = hg_before[f"gu{layer}"]
                with sp.Fori(0, NF) as i:
                    load_unit(w_gate_k[layer], i * CH, i * 16 + base)
                    load_unit(w_up_k[layer], i * CH, i * 16 + (base + 8))

            def down(layer):
                base = hg_before[f"down{layer}"]
                per = FB // 4
                for c0 in range(0, NC, 2):
                    for g in range(2 * per):
                        hg0 = base + c0 * FB // HG + 2 * g
                        back = 2 if g < 2 and c0 else 6
                        c = c0 + g // per
                        k = 4 * (g % per)
                        load(g % RAW, w_down_k[layer][:, k:k + 4, c * CH:(c + 1) * CH], hg0 - back)

            gate_up(0)
            down(0)
            base = hg_before["qkv"]
            load_unit(w_v_k, 0, base, after_down=True)
            load_unit(w_k_k, 0, base + 8)
            load_unit(w_q_k, 0, base + 16)
            with sp.Fori(1, NC) as i:
                load_unit(w_v_k, i * CH, i * 24 + base)
                load_unit(w_k_k, i * CH, i * 24 + (base + 8))
                load_unit(w_q_k, i * CH, i * 24 + (base + 16))
            with sp.Fori(0, NC) as i:
                load_unit(w_o_k, i * CH, i * 8 + hg_before["wo"])
            gate_up(1)
            down(1)
            for c in range(NC):
                sp.wait_ge(staged, batches["out"] + c + 1 - NC)
                sp.dma_start(out_tiles[:, :, c * CH:(c + 1) * CH], res[:, :, c * CH:(c + 1) * CH])\
                    .then_inc(stored, 16)
            sp.wait_ge(stored, 16 * NC)

        @block.gpsimd
        def _(pool):
            step = Tally(pool, pool_step)
            step.inc(nc.gpsimd.memset(ident[:, :], 0.0))
            step.inc(nc.gpsimd.memset(power[:, :], -0.5))
            step.wait()
            nc.gpsimd.affine_select(out=ident[:, :], in_=ident[:, :], compare_op=ALU.not_equal, fill=1.0,
                                    base=0, pattern=[[-1, P]], channel_multiplier=1).then_inc(ident_ready, 1)
            pool.wait_ge(ws_landed, 16)
            nc.gpsimd.affine_select(out=w_s_nat[:, :, :], in_=w_s_nat[:, :, :], compare_op=ALU.is_ge, fill=0.0,
                                    base=0, pattern=[[0, G], [-1, P]], channel_multiplier=1).then_inc(ws_masked, 1)

            def inverse_root(dst, src, scale, eps, done):
                step.inc(nc.gpsimd.tensor_scalar(dst, src, scale, eps, ALU.mult, ALU.add))
                step.wait()
                nc.gpsimd.tensor_tensor(dst, dst, power[:, 0:dst.shape[1]], ALU.pow).then_inc(done, 1)

            def norm(n):
                pool.wait_ge(ms_ready, n + 1)
                inverse_root(rstd[:, n, :], rstd[:, n, :], 1.0 / D, EPS, rstd_ready)

            norm(0)
            pool.wait_ge(mv_ready, 1)
            inverse_root(ln_rstd[:, :], ln_mv[:, :, 1], 1.0, EPS, ln_rstd_ready)
            norm(1)
            norm(2)
            step.inc(nc.gpsimd.memset(mask[:, :, :], 0.0))
            step.wait()
            for n in (0, 2):
                nc.gpsimd.affine_select(out=mask[:, n, :], in_=mask[:, n, :], compare_op=ALU.is_ge, fill=NEG,
                                        base=0, pattern=[[-1, P]], channel_multiplier=1).then_inc(mask_ready, 1)

            def head_norms(i):
                for n, (scale, eps) in enumerate(((1.0 / P, EPS), (1.0, EPS * P))):
                    pool.wait_ge(kq_ss, i * 2 + (n + 1))
                    src = head_ss[:, n, :, :].rearrange("p t h -> p (t h)")
                    dst = head_rs[:, n, :, :].rearrange("p t h -> p (t h)")
                    inverse_root(dst, src, scale, eps, kq_rs)

            for i in range(NC):
                head_norms(i)
            norm(3)

        @block.scalar
        def _(act):
            step = Tally(act, act_step)
            slot_n = list(slot_before["v"])

            def split(m, j, slot_count=None, gain=None):
                raw_slot = j // 2 % RAW
                if j % 2 == 0:
                    act.wait_ge(raw_landed[raw_slot], slot_count)
                if not (isinstance(m, int) and m < RING):
                    act.wait_ge(w_used, m - (RING - 1))
                src = raw[:, raw_slot, (j % 2) * HG:(j % 2 + 1) * HG, :]
                dst = w_hi[:, j % RING, :, :]
                if gain is None:
                    nc.scalar.activation(dst, src, ACT.Copy).then_inc(hi_split, 1)
                    return
                for k in range(HG):
                    kb = HG * (j % (KB // HG)) + k
                    ins = nc.scalar.activation(dst[:, k, :], src[:, k, :], ACT.Copy,
                                               scale=gains[:, gain + kb:gain + kb + 1])
                ins.then_inc(hi_split, 1)

            def unit(m0, counts, hooks, j0=0, n=KB // HG, gain=None):
                for j in range(n):
                    split(m0 + j, j0 + j, counts[j // 2], gain)
                    for work in hooks.get(j, ()):
                        work()

            def landed(units, i=None, per=1, n=0):
                return [((slot_n[s] + n + 1) * 16) if i is None else i * (16 * per) + (slot_n[s] + n + 1) * 16
                        for s in range(RAW)]

            def advance(units):
                for s in range(RAW):
                    slot_n[s] += units

            def lhs_hi_part(b, hi, kb, gain=None):
                act.wait_ge(transposed, b + 1)
                for j in range(2):
                    if gain is None:
                        dst = hi[:, bass.ds(kb + 2 * j, 2), :].rearrange("p k s -> p (k s)")
                        ins = nc.scalar.activation(dst, tr[j][:, :], ACT.Copy)
                    else:
                        for k in range(2):
                            kk = kb + 2 * j + k
                            ins = nc.scalar.activation(hi[:, kk, :], tr[j][:, k * S:(k + 1) * S], ACT.Copy,
                                                       scale=gains[:, gain + kk:gain + kk + 1])
                ins.then_inc(lhs_hi, 1)

            def save_chunk(n, c, b):
                act.wait_ge(staged, b + 1 - NC)
                nc.scalar.activation(res[:, :, c * CH:(c + 1) * CH], stage[:, :, :], ACT.Copy)
                step.inc(nc.scalar.activation(junk_b[:, :], stage[:, 0, :], ACT.Square,
                                              accum_out=sums[:, n, 0, c:c + 1]))
                step.wait()
                nc.scalar.activation(junk_b[:, :], stage[:, 1, :], ACT.Square,
                                     accum_out=sums[:, n, 1, c:c + 1]).then_inc(res_saved, 1)

            for n, v in enumerate((a_norm[0, :], kv_norm, b_norm[0, :], ffn_norm[0, :], ffn_norm[1, :])):
                act.dma_start(rows[n * KB:(n + 1) * KB, :], v.rearrange("(k p) -> k p", p=P)).then_inc(rows_landed, 16)
            act.dma_start(rows[5 * KB:6 * KB, :], a_b_s[0, :, :]).then_inc(rows_landed, 16)
            act.dma_start(w_s_nat[:, :, :], a_w_s[0, :, :, :].rearrange("g t s -> t g s")).then_inc(ws_landed, 16)
            act.dma_start(ln_gain[:, :], a_ln_g[0, :].partition_broadcast(P)).then_inc(ln_landed, 16)
            act.dma_start(ln_bias[:, :], a_ln_b[0, :].partition_broadcast(P)).then_inc(ln_landed, 16)
            act.dma_start(head_gain[:, 0:1], k_norm.rearrange("(p a) -> p a", a=1)).then_inc(hgain_landed, 16)
            act.dma_start(head_gain[:, 1:2], b_q_norm[0, :].rearrange("(p a) -> p a", a=1)).then_inc(hgain_landed, 16)
            act.wait_ge(rows_transposed, 1)
            nc.scalar.activation(gains[:, :], acc[2][0][:, 0:6 * KB], ACT.Copy).then_inc(gains_ready, 1)
            act.wait_ge(gains_ready, 1)

            for c in range(NC):
                lhs_hi_part(c, a_hi, HPC * c, A_NORM)
            def read_v(c):
                act.wait_ge(w_used, hg_before["v"] + 8 * (c + 1))
                act.wait_ge(rstd_ready, 1)
                for t in range(TT):
                    ins = nc.scalar.activation(v_nat[:, t, c * CH:(c + 1) * CH], acc[c % 2][t][:, :],
                                               ACT.Gelu_apprx_tanh, scale=rstd[:, 0, t:t + 1])
                ins.then_inc(v_ready, 1)

            def x_squares():
                for t in range(TT):
                    for c in range(NC):
                        act.wait_ge(x_landed[c], 16)
                    ins = nc.scalar.activation(junk_a[:, :], res[:, t, :], ACT.Square,
                                               accum_out=sums[:, 0, t, 0:1])
                    if t < TT - 1:
                        step.inc(ins)
                        step.wait()
                ins.then_inc(sums_ready, 1)

            for c in range(NC):
                unit(hg_before["v"] + 8 * c, landed(NC, n=c), {3: [lambda c=c: read_v(c - 1) if c else x_squares()]})
            advance(NC)

            def take_wsT():
                act.wait_ge(wsT_done, 1)
                for n, bank in enumerate((tr[0], tr[1], acc[2][0], acc[2][1])):
                    ins = nc.scalar.activation(w_sT[:, 4 * n:4 * n + 4, :].rearrange("p g s -> p (g s)"),
                                               bank[:, :], ACT.Copy)
                ins.then_inc(wsT_ready, 1)

            def read_u(c):
                act.wait_ge(w_used, hg_before["u"] + 8 * (c + 1))
                if c:
                    act.wait_ge(staged, c)
                for t in range(TT):
                    ins = nc.scalar.activation(u_nat[:, t, :], acc[c % 2][t][:, :],
                                               ACT.Gelu_apprx_tanh, scale=rstd[:, 0, t:t + 1])
                ins.then_inc(u_ready, 1)

            for c in range(NC):
                hooks = {3: [lambda c=c: read_u(c - 1)] if c else [lambda: read_v(NC - 1), take_wsT]}
                if c:
                    hooks[7] = [lambda c=c: lhs_hi_part(batches["gated"] + c - 1, g_hi, HPC * (c - 1))]
                unit(hg_before["u"] + 8 * c, landed(NC, n=c), hooks)
            advance(NC)

            for c in range(NC):
                hooks = {3: [lambda c=c: save_chunk(1, c - 1, batches["x1"] + c - 1) if c else read_u(NC - 1)],
                         7: [lambda c=c: lhs_hi_part(batches["x1"] + c - 1, a_hi, HPC * (c - 1), FFN0) if c
                             else lhs_hi_part(batches["gated"] + NC - 1, g_hi, HPC * (NC - 1))]}
                unit(hg_before["wout"] + 8 * c, landed(NC, n=c), hooks)
            advance(NC)

            def gate_up(layer, norm, last_save, last_lhs):
                base, b0 = hg_before[f"gu{layer}"], batches[f"h{layer}"]

                def read_gate(i):
                    act.wait_ge(w_used, i * 16 + (base + 8))
                    act.wait_ge(transposed, i + b0)
                    act.wait_ge(rstd_ready, norm + 1)
                    for t in range(TT):
                        ins = nc.scalar.activation(stage[:, t, :], acc[0][t][:, :], ACT.Silu,
                                                   scale=rstd[:, norm, t:t + 1])
                    ins.then_inc(silu_ready, 1)

                def body(i, first):
                    n = 0 if first else 2
                    gate_hooks = {3: [last_save] if first else [],
                                  7: [last_lhs] if first else
                                  [lambda: lhs_hi_part(i + (b0 - 1), h_hi, i * HPC - HPC)]}
                    ii = None if first else i
                    unit(i * 16 + base, landed(0, ii, 2, 0), gate_hooks)
                    unit(i * 16 + (base + 8), landed(0, ii, 2, 1), {3: [lambda: read_gate(i)]})

                body(0, True)
                with act.Fori(1, NF) as i:
                    body(i, False)
                advance(2 * NF)

            gate_up(0, 1, lambda: save_chunk(1, NC - 1, batches["x1"] + NC - 1),
                    lambda: lhs_hi_part(batches["x1"] + NC - 1, a_hi, HPC * (NC - 1), FFN0))

            def down(layer):
                base, b0 = hg_before[f"down{layer}"], batches["x2"]
                n = FB // HG
                for c in range(NC):
                    counts = []
                    if c % 2 == 0:
                        uses = [0] * RAW
                    for g in range(n // 2):
                        s = (c % 2 * (n // 2) + g) % RAW
                        uses[s] += 1
                        counts.append(16 * (slot_n[s] + uses[s]))
                    if c % 2:
                        for s in range(RAW):
                            slot_n[s] += uses[s]
                    if c == 0:
                        hooks = {7: [lambda: lhs_hi_part(batches[f"h{layer}"] + NF - 1, h_hi, HPC * (NF - 1))]}
                    elif layer == 0:
                        hooks = {3: [lambda c=c: save_chunk(2, c - 1, b0 + c - 1)],
                                 7: [lambda c=c: lhs_hi_part(b0 + c - 1, a_hi, HPC * (c - 1))]}
                    else:
                        hooks = {}
                    unit(base + n * c, counts, hooks, j0=c % 2 * n, n=n)

            down(0)

            base = hg_before["qkv"]

            def read_val(i):
                act.wait_ge(w_used, i * 24 + (base + 8))
                act.wait_ge(rstd_ready, 3)
                for t in range(TT):
                    ins = nc.scalar.activation(val[:, t, bass.ds(i * CH, CH)], acc[0][t][:, :], ACT.Copy,
                                               scale=rstd[:, 2, t:t + 1])
                ins.then_inc(val_ready, 1)

            def read_kq(i, n):
                act.wait_ge(w_used, i * 24 + (base + 16 + 8 * n))
                dst = (k_nat, q_nat)[n]
                for t in range(TT):
                    ins = nc.scalar.activation(dst[:, t, :, :].rearrange("p h d -> p (h d)"), acc[1 + n][t][:, :],
                                               ACT.Copy, scale=rstd[:, 2, t:t + 1])
                ins.then_inc(kq_raw, 1)
                act.wait_ge(kq_raw, i * 2 + (n + 1))
                if n == 0:
                    if not isinstance(i, int):
                        act.wait_ge(kq_ss, i * 2)
                else:
                    act.wait_ge(kq_ss, i * 2 + 1)
                nc.scalar.activation(sq_nat[:, :, :, :].rearrange("p t h d -> p (t h d)"),
                                     dst[:, :, :, :].rearrange("p t h d -> p (t h d)"), ACT.Square)\
                    .then_inc(kq_squared, 1)

            def take_kqT(i, n):
                act.wait_ge(kq_transposed, i * 2 + (n + 1))
                dst = (kT, qT)[n]
                for j in range(2):
                    ins = nc.scalar.activation(dst[:, 2 * j:2 * j + 2, :].rearrange("p h s -> p (h s)"),
                                               tr[j][:, :], ACT.Copy, scale=head_gain[:, n:n + 1])
                ins.then_inc(kq_ready, 1)

            def exps(i, h):
                act.wait_ge(maxed, i * HPC + (h + 1))
                for t, (a, b) in enumerate(((0, 1), (1, 3))):
                    ins = nc.scalar.activation(prob[:, a:b, :].rearrange("p n s -> p (n s)"),
                                               score[:, a:b, :].rearrange("p n s -> p (n s)"), ACT.Exp,
                                               bias=neg_max[:, t:t + 1], accum_out=row_sum[:, t:t + 1])
                ins.then_inc(exped, 1)

            def take_probT(i, h):
                act.wait_ge(probT_done, i * HPC + (h + 1))
                nc.scalar.activation(probT[:, :, :].rearrange("p n s -> p (n s)"), tr[1][:, 0:3 * P], ACT.Copy)\
                    .then_inc(probT_ready, 1)

            def o_hi_part(i):
                lhs_hi_part(i + batches["o"], o_hi, i * HPC)

            def attention_hooks(i):
                hooks = {7: [lambda: take_kqT(i, 0)], 9: [lambda: take_kqT(i, 1)]}
                for h in range(HPC):
                    for off, f in ((0, exps), (2, take_probT)):
                        hooks.setdefault(min(11 + 3 * h + off, 23), []).append(lambda h=h, f=f: f(i, h))
                hooks.setdefault(23, []).append(lambda: o_hi_part(i))
                return hooks

            def qkv_body(i, first):
                ii = None if first else i
                hooks = {} if first else attention_hooks(i - 1)
                hooks[3] = [lambda: save_chunk(2, NC - 1, batches["x2"] + NC - 1)] if first else [lambda: read_kq(i - 1, 1)]
                if first:
                    hooks[7] = [lambda: lhs_hi_part(batches["x2"] + NC - 1, a_hi, HPC * (NC - 1))]
                    act.wait_ge(hgain_landed, 32)
                hooks[11] = [lambda: read_val(i)] + hooks.get(11, [])
                hooks[19] = [lambda: read_kq(i, 0)] + hooks.get(19, [])
                for n, gain in enumerate((KV_NORM, KV_NORM, B_NORM)):
                    unit(i * 24 + (base + 8 * n), landed(0, ii, 3, n),
                         {j - 8 * n: f for j, f in hooks.items() if 8 * n <= j < 8 * n + 8}, gain=gain)

            qkv_body(0, True)
            with act.Fori(1, NC) as i:
                qkv_body(i, False)
            advance(3 * NC)

            for c in range(NC):
                if c == 0:
                    def last_attention():
                        read_kq(NC - 1, 1)
                        for n in range(2):
                            take_kqT(NC - 1, n)
                        for h in range(HPC):
                            exps(NC - 1, h)
                            take_probT(NC - 1, h)
                    hooks = {3: [last_attention, lambda: o_hi_part(NC - 1)]}
                else:
                    hooks = {3: [lambda c=c: save_chunk(3, c - 1, batches["x3"] + c - 1)],
                             7: [lambda c=c: lhs_hi_part(batches["x3"] + c - 1, a_hi, HPC * (c - 1), FFN1)]}
                unit(hg_before["wo"] + 8 * c, landed(NC, n=c), hooks)
            advance(NC)

            gate_up(1, 3, lambda: save_chunk(3, NC - 1, batches["x3"] + NC - 1),
                    lambda: lhs_hi_part(batches["x3"] + NC - 1, a_hi, HPC * (NC - 1), FFN1))
            down(1)

        @block.vector
        def _(dve):
            step = Tally(dve, dve_step)

            def split(m, j, gain=None):
                dve.wait_ge(hi_split, m + 1)
                src = raw[:, j // 2 % RAW, (j % 2) * HG:(j % 2 + 1) * HG, :]
                hi, lo = w_hi[:, j % RING, :, :].bitcast(F32), w_lo[:, j % RING, :, :]
                if gain is None:
                    nc.vector.tensor_tensor(lo, src, hi, ALU.subtract).then_inc(lo_split, 1)
                    return
                for k in range(HG):
                    kb = HG * (j % (KB // HG)) + k
                    ins = nc.vector.scalar_tensor_tensor(
                        out=lo[:, k, :], in0=src[:, k, :], scalar=gains[:, gain + kb:gain + kb + 1],
                        in1=hi[:, k, :], op0=ALU.mult, op1=ALU.subtract)
                ins.then_inc(lo_split, 1)

            def unit(m0, hooks, j0=0, n=KB // HG, gain=None):
                for j in range(n):
                    split(m0 + j, j0 + j, gain)
                    for work in hooks.get(j, ()):
                        work()

            def lhs_lo_part(b, hi, lo, kb, gain=None):
                dve.wait_ge(lhs_hi, b + 1)
                for j in range(2):
                    if gain is None:
                        h = hi[:, bass.ds(kb + 2 * j, 2), :].rearrange("p k s -> p (k s)").bitcast(F32)
                        dst = lo[:, bass.ds(kb + 2 * j, 2), :].rearrange("p k s -> p (k s)")
                        ins = nc.vector.tensor_tensor(dst, tr[j][:, :], h, ALU.subtract)
                    else:
                        for k in range(2):
                            kk = kb + 2 * j + k
                            ins = nc.vector.scalar_tensor_tensor(
                                out=lo[:, kk, :], in0=tr[j][:, k * S:(k + 1) * S],
                                scalar=gains[:, gain + kk:gain + kk + 1], in1=hi[:, kk, :].bitcast(F32),
                                op0=ALU.mult, op1=ALU.subtract)
                ins.then_inc(lhs_lo, 1)

            def add_residual(phase, n_hg, c, b, saved, in_place=False):
                dve.wait_ge(w_used, hg_before[phase] + n_hg * (c + 1))
                if not in_place:
                    dve.wait_ge(transposed, b)
                    if saved:
                        dve.wait_ge(res_saved, saved)
                for t in range(TT):
                    old = res[:, t, c * CH:(c + 1) * CH]
                    ins = nc.vector.tensor_tensor(old if in_place else stage[:, t, :], acc[c % 2][t][:, :], old,
                                                  ALU.add)
                ins.then_inc(staged, 1)

            def total_squares(n, saved):
                dve.wait_ge(res_saved, saved)
                nc.vector.tensor_reduce(rstd[:, n, :], sums[:, n, :, :], AX_X, ALU.add).then_inc(ms_ready, 1)

            dve.wait_ge(gains_ready, 1)
            for c in range(NC):
                lhs_lo_part(c, a_hi, a_lo, HPC * c, A_NORM)

            def x_squares():
                dve.wait_ge(sums_ready, 1)
                nc.vector.tensor_copy(rstd[:, 0, :], sums[:, 0, :, 0]).then_inc(ms_ready, 1)

            def v_stats(c):
                dve.wait_ge(v_ready, c + 1)
                for t in range(TT):
                    step.inc(nc.vector.bn_stats(ln_stats[:, t, c, :], v_nat[:, t, c * CH:(c + 1) * CH]))
                if c == NC - 1:
                    step.wait()
                    for t in range(TT):
                        ins = nc.vector.bn_aggr(ln_mv[:, t, :], ln_stats[:, t, :, :].rearrange("p c s -> p (c s)"))
                    ins.then_inc(mv_ready, 1)

            def layer_norm(c):
                dve.wait_ge(ln_rstd_ready, 1)
                dve.wait_ge(ln_landed, 32)
                part = slice(c * CH, (c + 1) * CH)
                for t in range(TT):
                    step.inc(nc.vector.tensor_scalar(v_nat[:, t, part], v_nat[:, t, part], ln_mv[:, t, 0:1],
                                                     ln_rstd[:, t:t + 1], ALU.subtract, ALU.mult))
                step.wait()
                for t in range(TT):
                    step.inc(nc.vector.tensor_tensor(v_nat[:, t, part], v_nat[:, t, part], ln_gain[:, part], ALU.mult))
                step.wait()
                for t in range(TT):
                    ins = nc.vector.tensor_tensor(v_nat[:, t, part], v_nat[:, t, part], ln_bias[:, part], ALU.add)
                ins.then_inc(ln_done, 1)

            def gate(c):
                dve.wait_ge(mixed, c + 1)
                dve.wait_ge(u_ready, c + 1)
                dve.wait_ge(transposed, batches["gated"] + c)
                for t in range(TT):
                    for g in range(HPC):
                        cols = slice(g * P, (g + 1) * P)
                        col = B_S + HPC * c + g
                        ins = nc.vector.scalar_tensor_tensor(
                            out=stage[:, t, cols], in0=tr[t][:, cols], scalar=gains[:, col:col + 1],
                            in1=u_nat[:, t, cols], op0=ALU.add, op1=ALU.mult)
                ins.then_inc(staged, 1)

            for c in range(NC):
                unit(hg_before["v"] + 8 * c, {3: [x_squares]} if c == 0 else {5: [lambda c=c: v_stats(c - 1)]})
            for c in range(NC):
                if c == 0:
                    hooks = {5: [lambda: v_stats(NC - 1)], 7: [lambda: layer_norm(0)]}
                else:
                    hooks = {5: [lambda c=c: layer_norm(c)],
                             7: [lambda c=c: gate(c - 1),
                                 lambda c=c: lhs_lo_part(batches["gated"] + c - 1, g_hi, g_lo, HPC * (c - 1))]}
                unit(hg_before["u"] + 8 * c, hooks)
            for c in range(NC):
                if c == 0:
                    hooks = {7: [lambda: gate(NC - 1),
                                 lambda: lhs_lo_part(batches["gated"] + NC - 1, g_hi, g_lo, HPC * (NC - 1))]}
                else:
                    hooks = {3: [lambda c=c: add_residual("wout", 8, c - 1, batches["x1"] + c - 1, c - 1)],
                             7: [lambda c=c: lhs_lo_part(batches["x1"] + c - 1, a_hi, a_lo, HPC * (c - 1), FFN0)]}
                unit(hg_before["wout"] + 8 * c, hooks)

            def gate_up(layer, norm, first_hooks):
                base, b0 = hg_before[f"gu{layer}"], batches[f"h{layer}"]

                def hidden(i, u_end):
                    dve.wait_ge(w_used, u_end)
                    dve.wait_ge(silu_ready, i + (NF * layer + 1))
                    for t in range(TT):
                        ins = nc.vector.scalar_tensor_tensor(
                            out=stage[:, t, :], in0=acc[1][t][:, :], scalar=rstd[:, norm, t:t + 1],
                            in1=stage[:, t, :], op0=ALU.mult, op1=ALU.mult)
                    ins.then_inc(staged, 1)

                def body(i, first):
                    hooks = first_hooks if first else {
                        3: [lambda: hidden(i - 1, i * 16 + base)],
                        7: [lambda: lhs_lo_part(i + (b0 - 1), h_hi, h_lo, i * HPC - HPC)]}
                    unit(i * 16 + base, hooks)
                    unit(i * 16 + (base + 8), {})

                body(0, True)
                with dve.Fori(1, NF) as i:
                    body(i, False)
                return hidden

            def down(layer, hidden):
                base = hg_before[f"down{layer}"]
                n = FB // HG
                for c in range(NC):
                    if c == 0:
                        b = batches[f"h{layer}"] + NF - 1
                        hooks = {3: [lambda: hidden(NF - 1, base)],
                                 7: [lambda: lhs_lo_part(b, h_hi, h_lo, HPC * (NF - 1))]}
                    elif layer == 0:
                        hooks = {3: [lambda c=c: add_residual("down0", n, c - 1, batches["x2"] + c - 1, NC + c - 1)],
                                 7: [lambda c=c: lhs_lo_part(batches["x2"] + c - 1, a_hi, a_lo, HPC * (c - 1))]}
                    else:
                        hooks = {3: [lambda c=c: add_residual("down1", n, c - 1, 0, 0, in_place=True)]}
                    unit(base + n * c, hooks, j0=c % 2 * n, n=n)

            hidden = gate_up(0, 1, {
                3: [lambda: add_residual("wout", 8, NC - 1, batches["x1"] + NC - 1, NC - 1)],
                7: [lambda: total_squares(1, NC),
                    lambda: lhs_lo_part(batches["x1"] + NC - 1, a_hi, a_lo, HPC * (NC - 1), FFN0)]})
            down(0, hidden)

            base = hg_before["qkv"]
            last_x2 = batches["x2"] + NC - 1

            def square_sums(i, n):
                dve.wait_ge(kq_squared, i * 2 + (n + 1))
                nc.vector.tensor_reduce(head_ss[:, n, :, :], sq_nat[:, :, :, :], AX_X, ALU.add).then_inc(kq_ss, 1)

            def norm_heads(i, n):
                dve.wait_ge(kq_rs, i * 2 + (n + 1))
                nat = (k_nat, q_nat)[n][:, :, :, :].rearrange("p t h d -> p (t h) d")
                rs = head_rs[:, n, :, :].rearrange("p t (h a) -> p (t h) a", a=1).to_broadcast([P, TT * HPC, P])
                nc.vector.tensor_tensor(nat, nat, rs, ALU.mult).then_inc(kq_normed, 1)

            def maxima(i, h):
                dve.wait_ge(scored, i * HPC + (h + 1))
                step.inc(nc.vector.tensor_tensor(score[:, :, :].rearrange("p n s -> p (n s)"), tr[0][:, 0:3 * P],
                                                 mask[:, :, :].rearrange("p n s -> p (n s)"), ALU.add))
                step.wait()
                for t, (a, b) in enumerate(((0, 1), (1, 3))):
                    ins = nc.vector.tensor_reduce(neg_max[:, t:t + 1], score[:, a:b, :].rearrange("p n s -> p (n s)"),
                                                  AX_X, ALU.max, negate=True)
                ins.then_inc(maxed, 1)

            def head_output(i, h):
                dve.wait_ge(exped, i * HPC + (h + 1))
                step.inc(nc.vector.reciprocal(row_inv[:, :], row_sum[:, :]))
                step.wait()
                dve.wait_ge(pv_done, i * HPC + (h + 1))
                if h == 0:
                    dve.wait_ge(transposed, i + batches["o"])
                    dve.wait_ge(res_saved, 2 * NC)
                for t in range(TT):
                    ins = nc.vector.tensor_scalar(stage[:, t, h * P:(h + 1) * P], tr[0][:, t * P:(t + 1) * P],
                                                  row_inv[:, t:t + 1], None, ALU.mult)
                ins.then_inc(staged if h == HPC - 1 else head_out, 1)

            def o_lo_part(i):
                lhs_lo_part(i + batches["o"], o_hi, o_lo, i * HPC)

            def attention_hooks(i):
                hooks = {4: [lambda: square_sums(i, 1)], 6: [lambda: norm_heads(i, 1)], 11: [lambda: maxima(i, 0)]}
                for h in range(HPC):
                    hooks[14 + 3 * h] = [lambda h=h: head_output(i, h)]
                    if h < HPC - 1:
                        hooks[14 + 3 * h].append(lambda h=h: maxima(i, h + 1))
                hooks[23].append(lambda: o_lo_part(i))
                return hooks

            def qkv_body(i, first):
                if first:
                    hooks = {3: [lambda: add_residual("down0", FB // HG, NC - 1, last_x2, 2 * NC - 1)],
                             7: [lambda: total_squares(2, 2 * NC),
                                 lambda: lhs_lo_part(last_x2, a_hi, a_lo, HPC * (NC - 1))]}
                else:
                    hooks = attention_hooks(i - 1)
                hooks[20] = [lambda: square_sums(i, 0)] + hooks.get(20, [])
                hooks[22] = [lambda: norm_heads(i, 0)]
                for n, gain in enumerate((KV_NORM, KV_NORM, B_NORM)):
                    unit(i * 24 + (base + 8 * n),
                         {j - 8 * n: f for j, f in hooks.items() if 8 * n <= j < 8 * n + 8}, gain=gain)

            qkv_body(0, True)
            dve.wait_ge(mask_ready, 2)
            with dve.Fori(1, NC) as i:
                step.enter(i, 2 * HPC, first=1)
                qkv_body(i, False)
                step.leave(NC)

            def last_attention():
                square_sums(NC - 1, 1)
                norm_heads(NC - 1, 1)
                for h in range(HPC):
                    maxima(NC - 1, h)
                    head_output(NC - 1, h)
                o_lo_part(NC - 1)

            for c in range(NC):
                if c == 0:
                    hooks = {3: [last_attention]}
                else:
                    hooks = {3: [lambda c=c: add_residual("wo", 8, c - 1, batches["x3"] + c - 1, 2 * NC + c - 1)],
                             7: [lambda c=c: lhs_lo_part(batches["x3"] + c - 1, a_hi, a_lo, HPC * (c - 1), FFN1)]}
                unit(hg_before["wo"] + 8 * c, hooks)
            hidden = gate_up(1, 3, {
                3: [lambda: add_residual("wo", 8, NC - 1, batches["x3"] + NC - 1, 3 * NC - 1)],
                7: [lambda: total_squares(3, 3 * NC),
                    lambda: lhs_lo_part(batches["x3"] + NC - 1, a_hi, a_lo, HPC * (NC - 1), FFN1)]})
            down(1, hidden)
            add_residual("down1", FB // HG, NC - 1, 0, 0, in_place=True)

        @block.tensor
        def _(pe):
            def unit(m0, hi, lo, s, hooks={}, lhs_waits={}, j0=0, n=KB // HG):
                for j in range(n):
                    if j in lhs_waits:
                        pe.wait_ge(lhs_lo, lhs_waits[j])
                    pe.wait_ge(lo_split, m0 + j + 1)
                    for k in range(HG):
                        kb, slot = HG * j + k, (j0 + j) % RING
                        first, last = kb == 0, kb == HG * n - 1
                        for t in range(TT):
                            tok = slice(t * P, (t + 1) * P)
                            nc.tensor.matmul(acc[s][t][:, :], hi[:, kb, tok], w_hi[:, slot, k, :],
                                             start=first, stop=False)
                            nc.tensor.matmul(acc[s][t][:, :], hi[:, kb, tok], w_lo[:, slot, k, :],
                                             start=False, stop=False)
                            ins = nc.tensor.matmul(acc[s][t][:, :], lo[:, kb, tok], w_hi[:, slot, k, :],
                                                   start=False, stop=last)
                    ins.then_inc(w_used, 1)
                    for work in hooks.get(j, ()):
                        work()

            def transpose_batch(b, src=None):
                if src is None:
                    pe.wait_ge(staged, b + 1 - NC)
                if not (isinstance(b, int) and b == 0):
                    pe.wait_ge(lhs_lo, b)
                for j in range(2):
                    for k in range(2):
                        for t in range(TT):
                            blk = slice((2 * j + k) * P, (2 * j + k + 1) * P)
                            from_ = stage[:, t, blk] if src is None else src[:, t, blk]
                            ins = nc.tensor.transpose(tr[j][:, k * S + t * P:k * S + (t + 1) * P], from_, ident[:, :])
                ins.then_inc(transposed, 1)

            pe.wait_ge(ident_ready, 1)
            pe.wait_ge(rows_landed, 6 * 16)
            nc.tensor.transpose(acc[2][0][:, 0:6 * KB], rows[:, :], ident[0:6 * KB, 0:6 * KB]).then_inc(rows_transposed, 1)
            for c in range(NC):
                pe.wait_ge(x_landed[c], 16)
                transpose_batch(c, res[:, :, c * CH:(c + 1) * CH])

            pe.wait_ge(lhs_lo, NC)
            unit(hg_before["v"], a_hi, a_lo, 0)
            unit(hg_before["v"] + 8, a_hi, a_lo, 1)
            with pe.Fori(1, NC // 2) as i:
                for s in range(2):
                    pe.wait_ge(v_ready, i * 2 + (s - 1))
                    unit(i * 16 + (hg_before["v"] + 8 * s), a_hi, a_lo, s)

            pe.wait_ge(ws_masked, 1)
            pe.wait_ge(gains_ready, 1)
            for n, bank in enumerate((tr[0], tr[1], acc[2][0], acc[2][1])):
                for g in range(4):
                    ins = nc.tensor.transpose(bank[:, g * P:(g + 1) * P], w_s_nat[:, 4 * n + g, :], ident[:, :])
            ins.then_inc(wsT_done, 1)

            def mix(c):
                pe.wait_ge(ln_done, c + 1)
                if c == 0:
                    pe.wait_ge(wsT_ready, 1)
                pe.wait_ge(lhs_lo, batches["gated"] + c)
                for t in range(TT):
                    for g in range(HPC):
                        gg = HPC * c + g
                        ins = nc.tensor.matmul(tr[t][:, g * P:(g + 1) * P], w_sT[:, gg, :],
                                               v_nat[:, t, gg * P:(gg + 1) * P], start=True, stop=True)
                ins.then_inc(mixed, 1)

            def gated_hooks(c):
                return {3: [lambda: mix(c)], 5: [lambda: transpose_batch(batches["gated"] + c)]}

            for c in range(NC):
                if c < 2:
                    pe.wait_ge(v_ready, NC - 1 + c)
                else:
                    pe.wait_ge(u_ready, c - 1)
                unit(hg_before["u"] + 8 * c, a_hi, a_lo, c % 2, gated_hooks(c - 1) if c else {})

            last = batches["gated"] + NC - 1
            pe.wait_ge(u_ready, NC - 1)
            unit(hg_before["wout"], g_hi, g_lo, 0, gated_hooks(NC - 1), {0: last, 6: last + 1})
            pe.wait_ge(u_ready, NC)
            unit(hg_before["wout"] + 8, g_hi, g_lo, 1, {3: [lambda: transpose_batch(batches["x1"])]})
            with pe.Fori(1, NC // 2) as i:
                for s in range(2):
                    pe.wait_ge(staged, i * 2 + (batches["x1"] - NC + s - 1))
                    unit(i * 16 + (hg_before["wout"] + 8 * s), g_hi, g_lo, s,
                         {3: [lambda s=s: transpose_batch(i * 2 + (batches["x1"] + s - 1))]})

            def gate_up(layer):
                base, b0 = hg_before[f"gu{layer}"], batches[f"h{layer}"]
                with pe.Fori(0, NF) as i:
                    pe.wait_ge(staged, i + (b0 - 1 - NC))
                    unit(i * 16 + base, a_hi, a_lo, 0, {3: [lambda: transpose_batch(i + (b0 - 1))]}, {0: b0 - 1, 6: b0})
                    pe.wait_ge(staged, i + (b0 - NC))
                    unit(i * 16 + (base + 8), a_hi, a_lo, 1)
                    pe.wait_ge(silu_ready, i + (NF * layer + 1))

            def down(layer):
                base, n = hg_before[f"down{layer}"], FB // HG
                b0 = batches["x2" if layer == 0 else "out"]
                unit(base, h_hi, h_lo, 0, {3: [lambda: transpose_batch(b0 - 1)]}, {0: b0 - 1, n - 2: b0}, n=n)
                pe.wait_ge(staged, b0 - NC)
                unit(base + n, h_hi, h_lo, 1, {3: [lambda: transpose_batch(b0)]} if layer == 0 else {}, j0=n, n=n)
                with pe.Fori(1, NC // 2) as i:
                    for s in range(2):
                        pe.wait_ge(staged, i * 2 + (b0 - NC + s - 1))
                        unit(i * 2 * n + (base + n * s), h_hi, h_lo, s,
                             {3: [lambda s=s: transpose_batch(i * 2 + (b0 + s - 1))]} if layer == 0 else {},
                             j0=n * s, n=n)

            gate_up(0)
            down(0)

            def transpose_heads(i, n):
                pe.wait_ge(kq_normed, i * 2 + (n + 1))
                if n == 0:
                    pe.wait_ge(lhs_lo, i + batches["o"])
                else:
                    pe.wait_ge(kq_ready, i * 2 + 1)
                nat = (k_nat, q_nat)[n]
                for h in range(HPC):
                    for t in range(TT):
                        at = h % 2 * S + t * P
                        ins = nc.tensor.transpose(tr[h // 2][:, at:at + P], nat[:, t, h, :], ident[:, :])
                ins.then_inc(kq_transposed, 1)

            def scores(i, h):
                if h == 0:
                    pe.wait_ge(kq_ready, i * 2 + 2)
                else:
                    pe.wait_ge(head_out, i * (HPC - 1) + h)
                nc.tensor.matmul(tr[0][:, 0:P], qT[:, h, 0:P], kT[:, h, 0:P], start=True, stop=True)
                nc.tensor.matmul(tr[0][:, P:3 * P], qT[:, h, P:2 * P], kT[:, h, 0:2 * P],
                                 start=True, stop=True).then_inc(scored, 1)

            def transpose_probs(i, h):
                pe.wait_ge(exped, i * HPC + (h + 1))
                for n in range(3):
                    ins = nc.tensor.transpose(tr[1][:, n * P:(n + 1) * P], prob[:, n, :], ident[:, :])
                ins.then_inc(probT_done, 1)

            def values(i, h):
                pe.wait_ge(probT_ready, i * HPC + (h + 1))
                if h == 0:
                    pe.wait_ge(val_ready, i + 1)
                v = [val[:, t, bass.ds(i * CH + h * P, P)] for t in range(TT)]
                nc.tensor.matmul(tr[0][:, 0:P], probT[:, 0, :], v[0], start=True, stop=True)
                nc.tensor.matmul(tr[0][:, P:2 * P], probT[:, 1, :], v[0], start=True, stop=False)
                nc.tensor.matmul(tr[0][:, P:2 * P], probT[:, 2, :], v[1], start=False, stop=True).then_inc(pv_done, 1)

            def attention_hooks(i):
                hooks = {3: [lambda: transpose_heads(i, 0)], 5: [lambda: transpose_heads(i, 1)], 7: [lambda: scores(i, 0)]}
                for h in range(HPC):
                    hooks[9 + 3 * h] = [lambda h=h: transpose_probs(i, h)]
                    hooks[10 + 3 * h] = [lambda h=h: values(i, h)]
                    if h < HPC - 1:
                        hooks[10 + 3 * h].append(lambda h=h: scores(i, h + 1))
                hooks[20] = [lambda: transpose_batch(i + batches["o"])]
                return hooks

            base = hg_before["qkv"]

            def qkv_body(i, hooks, lhs_waits):
                for n in range(3):
                    if not isinstance(i, int):
                        if n == 0:
                            pe.wait_ge(val_ready, i)
                        else:
                            pe.wait_ge(kq_raw, i * 2 + (n - 2))
                    elif n < 2:
                        pe.wait_ge(staged, batches["x2"] + 3 + n - NC)
                    unit(i * 24 + (base + 8 * n), a_hi, a_lo, n,
                         {j - 8 * n: f for j, f in hooks.items() if 8 * n <= j < 8 * n + 8}, lhs_waits if n == 0 else {})

            b_last = batches["x2"] + NC - 1
            qkv_body(0, {3: [lambda: transpose_batch(b_last)]}, {0: b_last, 6: b_last + 1})
            with pe.Fori(1, NC) as i:
                qkv_body(i, attention_hooks(i - 1), {})

            def last_attention():
                g = NC - 1
                transpose_heads(g, 1)
                for h in range(HPC):
                    scores(g, h)
                    transpose_probs(g, h)
                    values(g, h)
                transpose_batch(batches["o"] + g)

            last_o = batches["o"] + NC - 1
            pe.wait_ge(val_ready, NC)
            unit(hg_before["wo"], o_hi, o_lo, 0,
                 {1: [lambda: transpose_heads(NC - 1, 0)], 3: [last_attention]}, {0: last_o, 6: last_o + 1})
            pe.wait_ge(kq_raw, 2 * NC - 1)
            unit(hg_before["wo"] + 8, o_hi, o_lo, 1, {3: [lambda: transpose_batch(batches["x3"])]})
            with pe.Fori(1, NC // 2) as i:
                for s in range(2):
                    pe.wait_ge(staged, i * 2 + (batches["x3"] - NC + s - 1))
                    unit(i * 16 + (hg_before["wo"] + 8 * s), o_hi, o_lo, s,
                         {3: [lambda s=s: transpose_batch(i * 2 + (batches["x3"] + s - 1))]})
            gate_up(1)
            down(1)


_INS = ["x", "a_norm", "a_w_in", "a_ln_g", "a_ln_b", "a_w_s", "a_b_s", "a_w_out", "kv_norm", "w_k", "w_v", "k_norm",
        "b_norm", "b_w_q", "b_q_norm", "b_w_o", "ffn_norm", "ffn_w_gate", "ffn_w_up", "ffn_w_down"]


def kernel(**inputs):
    import numpy as _np
    import concourse.bacc as _bacc
    from concourse import mybir as _mybir
    from concourse.bass_utils import run_bass_kernel_spmd as _run

    nc = _bacc.Bacc("TRN2", target_bir_lowering=False, num_devices=1)
    arrays, args = {}, []
    for name in _INS:
        a = _np.ascontiguousarray(inputs[name])
        arrays[f"in_{name}_dram"] = a
        args.append(nc.dram_tensor(f"in_{name}_dram", a.shape, _mybir.dt.from_np(a.dtype), kind="ExternalInput").ap())
    shape = tuple(inputs["x"].shape)
    args.append(nc.dram_tensor("out_0_dram", shape, _mybir.dt.float32, kind="ExternalOutput").ap())
    yoco_kernel(nc, *args)
    r = _run(nc, [arrays], core_ids=[0])
    return r.results[0]["out_0_dram"]
```

```python
from contextlib import ExitStack

import concourse.bass as bass
from concourse import mybir

F32 = mybir.dt.float32
F32R = mybir.dt.float32r
ACT = mybir.ActivationFunctionType
ALU = mybir.AluOpType
AX_X = mybir.AxisListType.X

P = 128
CH = 512
HG = 2
RAW = 4
RING = 4
EPS = 1e-6
NEG = -1e30


class Tally:

    def __init__(self, engine, sem):
        self.engine, self.sem = engine, sem
        self.base = self.n = self.per = 0
        self.i = None

    def inc(self, instruction):
        instruction.then_inc(self.sem, 1)
        self.n += 1
        return instruction

    def wait(self):
        count = self.base + self.n
        self.engine.wait_ge(self.sem, count if self.i is None else self.i * self.per + count)

    def enter(self, i, per, first=0):
        self.base, self.n = self.base + self.n - first * per, 0
        self.i, self.per = i, per

    def leave(self, end):
        assert self.n == self.per, (self.n, self.per)
        self.base, self.n, self.i = self.base + self.per * end, 0, None


def yoco_kernel(nc, x, a_norm, a_w_in, a_ln_g, a_ln_b, a_w_s, a_b_s, a_w_out, kv_norm, w_k, w_v, k_norm,
                b_norm, b_w_q, b_q_norm, b_w_o, ffn_norm, ffn_w_gate, ffn_w_up, ffn_w_down, out):
    _, S, D = x.shape
    F = ffn_w_gate.shape[2]
    G = a_w_s.shape[1]
    TT = S // P
    KB = D // P
    FB = F // P
    NC = D // CH
    NF = F // CH
    HPC = CH // P
    assert TT == 2 and KB == 16 and NC == 4 and G == KB and HPC == 4 and k_norm.shape[0] == P
    assert a_w_s.shape[2] == P and FB % 4 == 0 and (2 * FB // HG) % RING == 0

    PHASES = [("v", NC, KB), ("u", NC, KB), ("wout", NC, KB), ("gu0", 2 * NF, KB), ("down0", NC, FB),
              ("qkv", 3 * NC, KB), ("wo", NC, KB), ("gu1", 2 * NF, KB), ("down1", NC, FB)]
    hg_before, slot_before = {}, {}
    hg, slots = 0, [0] * RAW
    for name, units, kb in PHASES:
        hg_before[name], slot_before[name] = hg, list(slots)
        hg += units * kb // HG
        per_body = (1 if kb == KB else 2) * kb // (2 * HG)
        for g in range(units * kb // (2 * HG)):
            slots[g % per_body % RAW] += 1
    batches = {"x": 0, "gated": NC, "x1": 2 * NC, "h0": 3 * NC, "x2": 3 * NC + NF, "o": 4 * NC + NF,
               "x3": 5 * NC + NF, "h1": 6 * NC + NF, "out": 6 * NC + 2 * NF}

    WO_FIRST = [(0, 0), (0, 1), (0, 2), (1, 0), (1, 1), (1, 2), (0, 3), (1, 3)]

    w_in_v = a_w_in[0, :, D:2 * D].rearrange("(k p) n -> p k n", p=P)
    w_in_u = a_w_in[0, :, 0:D].rearrange("(k p) n -> p k n", p=P)
    w_out_k = a_w_out[0, :, :].rearrange("(k p) n -> p k n", p=P)
    w_gate_k = [ffn_w_gate[n, :, :].rearrange("(k p) n -> p k n", p=P) for n in range(2)]
    w_up_k = [ffn_w_up[n, :, :].rearrange("(k p) n -> p k n", p=P) for n in range(2)]
    w_down_k = [ffn_w_down[n, :, :].rearrange("(k p) n -> p k n", p=P) for n in range(2)]
    w_v_k = w_v.rearrange("(k p) n -> p k n", p=P)
    w_k_k = w_k.rearrange("(k p) n -> p k n", p=P)
    w_q_k = b_w_q[0, :, :].rearrange("(k p) n -> p k n", p=P)
    w_o_k = b_w_o[0, :, :].rearrange("(k p) n -> p k n", p=P)
    x_tiles = x[0, :, :].rearrange("(t p) n -> p t n", p=P)
    out_tiles = out[0, :, :].rearrange("(t p) n -> p t n", p=P)

    with ExitStack() as ctx:
        def sb(name, shape, dt, scope=ctx):
            return scope.enter_context(nc.sbuf_tensor(name, shape, dt))

        def sem(name):
            return ctx.enter_context(nc.semaphore(name))

        raw = sb("raw", [P, RAW, 2 * HG, CH], F32)
        w_hi = sb("w_hi", [P, RING, HG, CH], F32R)
        w_lo = sb("w_lo", [P, RING, HG, CH], F32R)
        a_hi = sb("a_hi", [P, KB, S], F32R)
        a_lo = sb("a_lo", [P, KB, S], F32R)
        res = sb("res", [P, TT, D], F32)
        stage = sb("stage", [P, TT, CH], F32)
        ident = sb("ident", [P, P], F32)
        junk_b = sb("junk_b", [P, CH], mybir.dt.bfloat16)
        gains = sb("gains", [P, 6 * KB], F32)
        head_gain = sb("head_gain", [P, 2], F32)
        sums = sb("sums", [P, 4, TT, NC], F32)
        rstd = sb("rstd", [P, 4, TT], F32)
        power = sb("power", [P, 8], F32)
        ln_stats = sb("ln_stats", [P, TT, NC, 6], F32)
        ln_mv = sb("ln_mv", [P, TT, 2], F32)
        ln_rstd = sb("ln_rstd", [P, TT], F32)
        head_ss = sb("head_ss", [P, 2, TT, HPC], F32)
        head_rs = sb("head_rs", [P, 2, TT, HPC], F32)
        neg_max = sb("neg_max", [P, TT], F32)
        row_sum = sb("row_sum", [P, TT], F32)
        row_inv = sb("row_inv", [P, TT], F32)
        A_NORM, KV_NORM, B_NORM, FFN0, FFN1, B_S = (n * KB for n in range(6))

        with ExitStack() as part:
            g_hi = sb("g_hi", [P, KB, S], F32R, part)
            g_lo = sb("g_lo", [P, KB, S], F32R, part)
            v_nat = sb("v_nat", [P, TT, D], F32, part)
            ln_gain = sb("ln_gain", [P, D], F32, part)
            ln_bias = sb("ln_bias", [P, D], F32, part)
            w_sT = sb("w_sT", [P, G, P], F32, part)
            u_nat = sb("u_nat", [P, TT, CH], F32, part)
        with ExitStack() as part:
            w_s_nat = sb("w_s_nat", [P, G, P], F32, part)
            junk_a = sb("junk_a", [P, D], F32, part)
            rows = sb("rows", [6 * KB, P], F32, part)
        with ExitStack() as part:
            h_hi = sb("h_hi", [P, FB, S], F32R, part)
            h_lo = sb("h_lo", [P, FB, S], F32R, part)
        with ExitStack() as part:
            o_hi = sb("o_hi", [P, KB, S], F32R, part)
            o_lo = sb("o_lo", [P, KB, S], F32R, part)
            val = sb("val", [P, TT, D], F32, part)
            k_nat = sb("k_nat", [P, TT, HPC, P], F32, part)
            q_nat = sb("q_nat", [P, TT, HPC, P], F32, part)
            kT = sb("kT", [P, HPC, S], F32, part)
            qT = sb("qT", [P, HPC, S], F32, part)
            sq_nat = sb("sq_nat", [P, TT, HPC, P], F32, part)
            mask = sb("mask", [P, 3, P], F32, part)
            score = sb("score", [P, 3, P], F32, part)
            prob = sb("prob", [P, 3, P], F32, part)
            probT = sb("probT", [P, 3, P], F32, part)

        acc = [[ctx.enter_context(nc.psum_tensor(f"acc{s}_{t}", [P, CH], F32)) for t in range(TT)] for s in range(3)]
        tr = [ctx.enter_context(nc.psum_tensor(f"tr{j}", [P, CH], F32)) for j in range(2)]

        x_banks = [tr, acc[2], acc[1], tr]

        raw_landed = [sem(f"raw_landed{s}") for s in range(RAW)]
        hi_split = sem("hi_split")
        lo_split = sem("lo_split")
        w_used = sem("w_used")
        staged = sem("staged")
        transposed = sem("transposed")
        lhs_hi = sem("lhs_hi")
        lhs_lo = sem("lhs_lo")
        res_saved = sem("res_saved")
        x_landed = [sem(f"x_landed{c}") for c in range(NC)]
        rows_landed, ws_landed, ln_landed = sem("rows_landed"), sem("ws_landed"), sem("ln_landed")
        hgain_landed = sem("hgain_landed")
        ident_ready, mask_ready, ws_masked = sem("ident_ready"), sem("mask_ready"), sem("ws_masked")
        rows_transposed, gains_ready = sem("rows_transposed"), sem("gains_ready")
        sums_ready = sem("sums_ready")
        ms_ready = sem("ms_ready")
        rstd_ready = sem("rstd_ready")
        wsT_done, wsT_ready = sem("wsT_done"), sem("wsT_ready")
        v_ready, mv_ready, ln_rstd_ready, ln_done = sem("v_ready"), sem("mv_ready"), sem("ln_rstd_ready"), sem("ln_done")
        u_ready, mixed = sem("u_ready"), sem("mixed")
        silu_ready = sem("silu_ready")
        val_ready = sem("val_ready")
        kq_raw, kq_squared, kq_ss, kq_rs = sem("kq_raw"), sem("kq_squared"), sem("kq_ss"), sem("kq_rs")
        kq_normed, kq_transposed, kq_ready = sem("kq_normed"), sem("kq_transposed"), sem("kq_ready")
        scored, maxed, exped = sem("scored"), sem("maxed"), sem("exped")
        probT_done, probT_ready, pv_done, head_out = sem("probT_done"), sem("probT_ready"), sem("pv_done"), sem("head_out")
        pool_step, act_step, dve_step = sem("pool_step"), sem("act_step"), sem("dve_step")
        stored = sem("stored")

        block = ctx.enter_context(nc.Block())

        @block.sync
        def _(sp):
            def load(slot, src, prev_hg):
                if prev_hg is not None:
                    sp.wait_ge(lo_split, prev_hg)
                sp.dma_start(raw[:, slot, :, :], src).then_inc(raw_landed[slot], 16)

            def load_unit(w, col, hg0, after_down=False):
                for j in range(KB // 4):
                    back = 2 if after_down and j < 2 else 6
                    load(j, w[:, 4 * j:4 * j + 4, bass.ds(col, CH)], hg0 + 2 * j - back)

            for n, v in enumerate((a_norm[0, :], kv_norm, b_norm[0, :], ffn_norm[0, :], ffn_norm[1, :])):
                sp.dma_start(rows[n * KB:(n + 1) * KB, :], v.rearrange("(k p) -> k p", p=P)).then_inc(rows_landed, 16)
            sp.dma_start(rows[5 * KB:6 * KB, :], a_b_s[0, :, :]).then_inc(rows_landed, 16)

            def load_x(c):
                sp.dma_start(res[:, :, c * CH:(c + 1) * CH], x_tiles[:, :, c * CH:(c + 1) * CH])\
                    .then_inc(x_landed[c], 16)

            for j, chunks in enumerate(((0,), (1, 2), (3,), ())):
                for c in chunks:
                    load_x(c)
                load(j, w_in_v[:, 4 * j:4 * j + 4, 0:CH], None)
            with sp.Fori(1, NC) as i:
                load_unit(w_in_v, i * CH, i * 8)
            with sp.Fori(0, NC) as i:
                load_unit(w_in_u, i * CH, i * 8 + hg_before["u"])
            with sp.Fori(0, NC) as i:
                load_unit(w_out_k, i * CH, i * 8 + hg_before["wout"])

            def gate_up(layer):
                base = hg_before[f"gu{layer}"]
                with sp.Fori(0, NF) as i:
                    load_unit(w_gate_k[layer], i * CH, i * 16 + base)
                    load_unit(w_up_k[layer], i * CH, i * 16 + (base + 8))

            def down(layer):
                base = hg_before[f"down{layer}"]
                per = FB // 4
                for c0 in range(0, NC, 2):
                    for g in range(2 * per):
                        hg0 = base + c0 * FB // HG + 2 * g
                        back = 2 if g < 2 and c0 else 6
                        c = c0 + g // per
                        k = 4 * (g % per)
                        load(g % RAW, w_down_k[layer][:, k:k + 4, c * CH:(c + 1) * CH], hg0 - back)

            gate_up(0)
            down(0)
            base = hg_before["qkv"]
            load_unit(w_v_k, 0, base, after_down=True)
            load_unit(w_k_k, 0, base + 8)
            load_unit(w_q_k, 0, base + 16)
            with sp.Fori(1, NC) as i:
                load_unit(w_v_k, i * CH, i * 24 + base)
                load_unit(w_k_k, i * CH, i * 24 + (base + 8))
                load_unit(w_q_k, i * CH, i * 24 + (base + 16))
            for n, (c, g) in enumerate(WO_FIRST):
                load(n % RAW, w_o_k[:, 4 * g:4 * g + 4, c * CH:(c + 1) * CH], hg_before["wo"] + 2 * n - 6)
            with sp.Fori(2, NC) as i:
                load_unit(w_o_k, i * CH, i * 8 + hg_before["wo"])
            gate_up(1)
            down(1)
            for c in range(NC):
                sp.wait_ge(staged, batches["out"] + c + 1 - NC)
                sp.dma_start(out_tiles[:, :, c * CH:(c + 1) * CH], res[:, :, c * CH:(c + 1) * CH])\
                    .then_inc(stored, 16)
            sp.wait_ge(stored, 16 * NC)

        @block.gpsimd
        def _(pool):
            step = Tally(pool, pool_step)
            step.inc(nc.gpsimd.memset(ident[:, :], 0.0))
            step.inc(nc.gpsimd.memset(power[:, :], -0.5))
            step.wait()
            nc.gpsimd.affine_select(out=ident[:, :], in_=ident[:, :], compare_op=ALU.not_equal, fill=1.0,
                                    base=0, pattern=[[-1, P]], channel_multiplier=1).then_inc(ident_ready, 1)
            pool.wait_ge(ws_landed, 16)
            nc.gpsimd.affine_select(out=w_s_nat[:, :, :], in_=w_s_nat[:, :, :], compare_op=ALU.is_ge, fill=0.0,
                                    base=0, pattern=[[0, G], [-1, P]], channel_multiplier=1).then_inc(ws_masked, 1)

            def inverse_root(dst, src, scale, eps, done):
                step.inc(nc.gpsimd.tensor_scalar(dst, src, scale, eps, ALU.mult, ALU.add))
                step.wait()
                nc.gpsimd.tensor_tensor(dst, dst, power[:, 0:dst.shape[1]], ALU.pow).then_inc(done, 1)

            def norm(n):
                pool.wait_ge(ms_ready, n + 1)
                inverse_root(rstd[:, n, :], rstd[:, n, :], 1.0 / D, EPS, rstd_ready)

            norm(0)
            pool.wait_ge(mv_ready, 1)
            inverse_root(ln_rstd[:, :], ln_mv[:, :, 1], 1.0, EPS, ln_rstd_ready)
            norm(1)
            norm(2)
            step.inc(nc.gpsimd.memset(mask[:, :, :], 0.0))
            step.wait()
            for n in (0, 2):
                nc.gpsimd.affine_select(out=mask[:, n, :], in_=mask[:, n, :], compare_op=ALU.is_ge, fill=NEG,
                                        base=0, pattern=[[-1, P]], channel_multiplier=1).then_inc(mask_ready, 1)

            def head_norms(i):
                for n, (scale, eps) in enumerate(((1.0 / P, EPS), (1.0, EPS * P))):
                    pool.wait_ge(kq_ss, i * 2 + (n + 1))
                    src = head_ss[:, n, :, :].rearrange("p t h -> p (t h)")
                    dst = head_rs[:, n, :, :].rearrange("p t h -> p (t h)")
                    inverse_root(dst, src, scale, eps, kq_rs)

            for i in range(NC):
                head_norms(i)
            norm(3)

        @block.scalar
        def _(act):
            step = Tally(act, act_step)

            def split(m, j, slot_count=None, gain=None):
                raw_slot = j // 2 % RAW
                if j % 2 == 0:
                    act.wait_ge(raw_landed[raw_slot], slot_count)
                if not (isinstance(m, int) and m < RING):
                    act.wait_ge(w_used, m - (RING - 1))
                src = raw[:, raw_slot, (j % 2) * HG:(j % 2 + 1) * HG, :]
                dst = w_hi[:, j % RING, :, :]
                if gain is None:
                    nc.scalar.activation(dst, src, ACT.Copy).then_inc(hi_split, 1)
                    return
                for k in range(HG):
                    kb = HG * (j % (KB // HG)) + k
                    ins = nc.scalar.activation(dst[:, k, :], src[:, k, :], ACT.Copy,
                                               scale=gains[:, gain + kb:gain + kb + 1])
                ins.then_inc(hi_split, 1)

            def unit(m0, counts, hooks, j0=0, n=KB // HG, gain=None):
                for j in range(n):
                    split(m0 + j, j0 + j, counts[j // 2], gain)
                    for work in hooks.get(j, ()):
                        work()

            def landed(phase, n, i=None, per=1):
                counts = [(slot_before[phase][s] + n + 1) * 16 for s in range(RAW)]
                return counts if i is None else [i * (16 * per) + count for count in counts]

            def lhs_hi_part(b, hi, kb, gain=None, banks=tr):
                act.wait_ge(transposed, b + 1)
                for j in range(2):
                    if gain is None:
                        dst = hi[:, bass.ds(kb + 2 * j, 2), :].rearrange("p k s -> p (k s)")
                        ins = nc.scalar.activation(dst, banks[j][:, :], ACT.Copy)
                    else:
                        for k in range(2):
                            kk = kb + 2 * j + k
                            ins = nc.scalar.activation(hi[:, kk, :], banks[j][:, k * S:(k + 1) * S], ACT.Copy,
                                                       scale=gains[:, gain + kk:gain + kk + 1])
                ins.then_inc(lhs_hi, 1)

            def save_chunk(n, c, b):
                act.wait_ge(staged, b + 1 - NC)
                nc.scalar.activation(res[:, :, c * CH:(c + 1) * CH], stage[:, :, :], ACT.Copy)
                step.inc(nc.scalar.activation(junk_b[:, :], stage[:, 0, :], ACT.Square,
                                              accum_out=sums[:, n, 0, c:c + 1]))
                step.wait()
                nc.scalar.activation(junk_b[:, :], stage[:, 1, :], ACT.Square,
                                     accum_out=sums[:, n, 1, c:c + 1]).then_inc(res_saved, 1)

            act.dma_start(head_gain[:, 0:1], k_norm.rearrange("(p a) -> p a", a=1)).then_inc(hgain_landed, 16)
            act.dma_start(head_gain[:, 1:2], b_q_norm[0, :].rearrange("(p a) -> p a", a=1)).then_inc(hgain_landed, 16)
            act.wait_ge(rows_transposed, 1)
            nc.scalar.activation(gains[:, :], acc[0][0][:, 0:6 * KB], ACT.Copy).then_inc(gains_ready, 1)
            act.wait_ge(gains_ready, 1)

            def x_hi_part(c):
                lhs_hi_part(c, a_hi, HPC * c, A_NORM, x_banks[c])

            def read_v(c):
                act.wait_ge(w_used, hg_before["v"] + 8 * (c + 1))
                act.wait_ge(rstd_ready, 1)
                for t in range(TT):
                    ins = nc.scalar.activation(v_nat[:, t, c * CH:(c + 1) * CH], acc[c % 2][t][:, :],
                                               ACT.Gelu_apprx_tanh, scale=rstd[:, 0, t:t + 1])
                ins.then_inc(v_ready, 1)

            def x_squares():
                act.dma_start(w_s_nat[:, :, :], a_w_s[0, :, :, :].rearrange("g t s -> t g s")).then_inc(ws_landed, 16)
                act.dma_start(ln_gain[:, :], a_ln_g[0, :].partition_broadcast(P)).then_inc(ln_landed, 16)
                act.dma_start(ln_bias[:, :], a_ln_b[0, :].partition_broadcast(P)).then_inc(ln_landed, 16)
                for t in range(TT):
                    for c in range(NC):
                        act.wait_ge(x_landed[c], 16)
                    ins = nc.scalar.activation(junk_a[:, :], res[:, t, :], ACT.Square,
                                               accum_out=sums[:, 0, t, 0:1])
                    if t < TT - 1:
                        step.inc(ins)
                        step.wait()
                ins.then_inc(sums_ready, 1)

            x_hi_part(0)
            for c in range(NC):
                hooks = {3: [lambda c=c: read_v(c - 1)]} if c else {
                    0: [lambda: x_hi_part(1)], 1: [lambda: x_hi_part(2)], 2: [lambda: x_hi_part(3)], 3: [x_squares]}
                unit(hg_before["v"] + 8 * c, landed("v", c), hooks)

            def take_wsT():
                act.wait_ge(wsT_done, 1)
                for n, bank in enumerate((tr[0], tr[1], acc[2][0], acc[2][1])):
                    ins = nc.scalar.activation(w_sT[:, 4 * n:4 * n + 4, :].rearrange("p g s -> p (g s)"),
                                               bank[:, :], ACT.Copy)
                ins.then_inc(wsT_ready, 1)

            def read_u(c):
                act.wait_ge(w_used, hg_before["u"] + 8 * (c + 1))
                if c:
                    act.wait_ge(staged, c)
                for t in range(TT):
                    ins = nc.scalar.activation(u_nat[:, t, :], acc[c % 2][t][:, :],
                                               ACT.Gelu_apprx_tanh, scale=rstd[:, 0, t:t + 1])
                ins.then_inc(u_ready, 1)

            for c in range(NC):
                hooks = {3: [lambda c=c: read_u(c - 1)] if c else [lambda: read_v(NC - 1), take_wsT]}
                if c:
                    hooks[7] = [lambda c=c: lhs_hi_part(batches["gated"] + c - 1, g_hi, HPC * (c - 1))]
                unit(hg_before["u"] + 8 * c, landed("u", c), hooks)

            for c in range(NC):
                hooks = {3: [lambda c=c: save_chunk(1, c - 1, batches["x1"] + c - 1) if c else read_u(NC - 1)],
                         7: [lambda c=c: lhs_hi_part(batches["x1"] + c - 1, a_hi, HPC * (c - 1), FFN0) if c
                             else lhs_hi_part(batches["gated"] + NC - 1, g_hi, HPC * (NC - 1))]}
                unit(hg_before["wout"] + 8 * c, landed("wout", c), hooks)

            def gate_up(layer, norm, last_save, last_lhs):
                base, b0 = hg_before[f"gu{layer}"], batches[f"h{layer}"]

                def read_gate(i):
                    act.wait_ge(w_used, i * 16 + (base + 8))
                    act.wait_ge(transposed, i + b0)
                    act.wait_ge(rstd_ready, norm + 1)
                    for t in range(TT):
                        ins = nc.scalar.activation(stage[:, t, :], acc[0][t][:, :], ACT.Silu,
                                                   scale=rstd[:, norm, t:t + 1])
                    ins.then_inc(silu_ready, 1)

                def body(i, first):
                    gate_hooks = {3: [last_save] if first else [],
                                  7: [last_lhs] if first else
                                  [lambda: lhs_hi_part(i + (b0 - 1), h_hi, i * HPC - HPC)]}
                    ii = None if first else i
                    unit(i * 16 + base, landed(f"gu{layer}", 0, ii, 2), gate_hooks)
                    unit(i * 16 + (base + 8), landed(f"gu{layer}", 1, ii, 2), {3: [lambda: read_gate(i)]})

                body(0, True)
                with act.Fori(1, NF) as i:
                    body(i, False)

            gate_up(0, 1, lambda: save_chunk(1, NC - 1, batches["x1"] + NC - 1),
                    lambda: lhs_hi_part(batches["x1"] + NC - 1, a_hi, HPC * (NC - 1), FFN0))

            def down(layer):
                base, b0 = hg_before[f"down{layer}"], batches["x2"]
                n = FB // HG
                groups = list(slot_before[f"down{layer}"])
                for c in range(NC):
                    counts = []
                    for g in range(n // 2):
                        s = (c % 2 * (n // 2) + g) % RAW
                        groups[s] += 1
                        counts.append(16 * groups[s])
                    if c == 0:
                        hooks = {7: [lambda: lhs_hi_part(batches[f"h{layer}"] + NF - 1, h_hi, HPC * (NF - 1))]}
                    elif layer == 0:
                        hooks = {3: [lambda c=c: save_chunk(2, c - 1, b0 + c - 1)],
                                 7: [lambda c=c: lhs_hi_part(b0 + c - 1, a_hi, HPC * (c - 1))]}
                    else:
                        hooks = {}
                    unit(base + n * c, counts, hooks, j0=c % 2 * n, n=n)

            down(0)

            base = hg_before["qkv"]

            def read_val(i):
                act.wait_ge(w_used, i * 24 + (base + 8))
                act.wait_ge(rstd_ready, 3)
                for t in range(TT):
                    ins = nc.scalar.activation(val[:, t, bass.ds(i * CH, CH)], acc[0][t][:, :], ACT.Copy,
                                               scale=rstd[:, 2, t:t + 1])
                ins.then_inc(val_ready, 1)

            def read_kq(i, n):
                act.wait_ge(w_used, i * 24 + (base + 16 + 8 * n))
                dst = (k_nat, q_nat)[n]
                for t in range(TT):
                    ins = nc.scalar.activation(dst[:, t, :, :].rearrange("p h d -> p (h d)"), acc[1 + n][t][:, :],
                                               ACT.Copy, scale=rstd[:, 2, t:t + 1])
                ins.then_inc(kq_raw, 1)
                act.wait_ge(kq_raw, i * 2 + (n + 1))
                if n == 0:
                    if not isinstance(i, int):
                        act.wait_ge(kq_ss, i * 2)
                else:
                    act.wait_ge(kq_ss, i * 2 + 1)
                nc.scalar.activation(sq_nat[:, :, :, :].rearrange("p t h d -> p (t h d)"),
                                     dst[:, :, :, :].rearrange("p t h d -> p (t h d)"), ACT.Square)\
                    .then_inc(kq_squared, 1)

            def take_kqT(i, n):
                act.wait_ge(kq_transposed, i * 2 + (n + 1))
                dst = (kT, qT)[n]
                for j in range(2):
                    ins = nc.scalar.activation(dst[:, 2 * j:2 * j + 2, :].rearrange("p h s -> p (h s)"),
                                               tr[j][:, :], ACT.Copy, scale=head_gain[:, n:n + 1])
                ins.then_inc(kq_ready, 1)

            def exps(i, h):
                act.wait_ge(maxed, i * HPC + (h + 1))
                for t, (a, b) in enumerate(((0, 1), (1, 3))):
                    ins = nc.scalar.activation(prob[:, a:b, :].rearrange("p n s -> p (n s)"),
                                               score[:, a:b, :].rearrange("p n s -> p (n s)"), ACT.Exp,
                                               bias=neg_max[:, t:t + 1], accum_out=row_sum[:, t:t + 1])
                ins.then_inc(exped, 1)

            def take_probT(i, h):
                act.wait_ge(probT_done, i * HPC + (h + 1))
                nc.scalar.activation(probT[:, :, :].rearrange("p n s -> p (n s)"), tr[1][:, 0:3 * P], ACT.Copy)\
                    .then_inc(probT_ready, 1)

            def o_hi_part(i):
                lhs_hi_part(i + batches["o"], o_hi, i * HPC)

            def attention_hooks(i):
                hooks = {7: [lambda: take_kqT(i, 0)], 9: [lambda: take_kqT(i, 1)]}
                for h in range(HPC):
                    for off, f in ((0, exps), (2, take_probT)):
                        hooks.setdefault(min(11 + 3 * h + off, 23), []).append(lambda h=h, f=f: f(i, h))
                hooks.setdefault(23, []).append(lambda: o_hi_part(i))
                return hooks

            def qkv_body(i, first):
                ii = None if first else i
                hooks = {} if first else attention_hooks(i - 1)
                hooks[3] = [lambda: save_chunk(2, NC - 1, batches["x2"] + NC - 1)] if first else [lambda: read_kq(i - 1, 1)]
                if first:
                    hooks[7] = [lambda: lhs_hi_part(batches["x2"] + NC - 1, a_hi, HPC * (NC - 1))]
                    act.wait_ge(hgain_landed, 32)
                hooks[11] = [lambda: read_val(i)] + hooks.get(11, [])
                hooks[19] = hooks.get(19, []) + [lambda: read_kq(i, 0)]
                for n, gain in enumerate((KV_NORM, KV_NORM, B_NORM)):
                    unit(i * 24 + (base + 8 * n), landed("qkv", n, ii, 3),
                         {j - 8 * n: f for j, f in hooks.items() if 8 * n <= j < 8 * n + 8}, gain=gain)

            qkv_body(0, True)
            with act.Fori(1, NC) as i:
                qkv_body(i, False)

            g = NC - 1
            hooks = {2: [lambda: read_kq(g, 1)], 4: [lambda: take_kqT(g, 0)], 5: [lambda: take_kqT(g, 1)]}
            for h in range(HPC):
                hooks[6 + 2 * h] = [lambda h=h: exps(g, h)]
                hooks[7 + 2 * h] = [lambda h=h: take_probT(g, h)]
            hooks[14] = [lambda: o_hi_part(g)]
            unit(hg_before["wo"], landed("wo", 0) + landed("wo", 1), hooks, n=16)

            def x3(c):
                return [lambda: save_chunk(3, c, batches["x3"] + c)]

            def x3_hi(c):
                return [lambda: lhs_hi_part(batches["x3"] + c, a_hi, HPC * c, FFN1)]

            unit(hg_before["wo"] + 16, landed("wo", 2), {1: x3(0), 7: x3_hi(0) + x3(1)})
            unit(hg_before["wo"] + 24, landed("wo", 3), {3: x3_hi(1) + x3(2), 7: x3_hi(2)})

            gate_up(1, 3, lambda: save_chunk(3, NC - 1, batches["x3"] + NC - 1),
                    lambda: lhs_hi_part(batches["x3"] + NC - 1, a_hi, HPC * (NC - 1), FFN1))
            down(1)

        @block.vector
        def _(dve):
            step = Tally(dve, dve_step)

            def split(m, j, gain=None):
                dve.wait_ge(hi_split, m + 1)
                src = raw[:, j // 2 % RAW, (j % 2) * HG:(j % 2 + 1) * HG, :]
                hi, lo = w_hi[:, j % RING, :, :].bitcast(F32), w_lo[:, j % RING, :, :]
                if gain is None:
                    nc.vector.tensor_tensor(lo, src, hi, ALU.subtract).then_inc(lo_split, 1)
                    return
                for k in range(HG):
                    kb = HG * (j % (KB // HG)) + k
                    ins = nc.vector.scalar_tensor_tensor(
                        out=lo[:, k, :], in0=src[:, k, :], scalar=gains[:, gain + kb:gain + kb + 1],
                        in1=hi[:, k, :], op0=ALU.mult, op1=ALU.subtract)
                ins.then_inc(lo_split, 1)

            def unit(m0, hooks, j0=0, n=KB // HG, gain=None):
                for j in range(n):
                    split(m0 + j, j0 + j, gain)
                    for work in hooks.get(j, ()):
                        work()

            def lhs_lo_part(b, hi, lo, kb, gain=None, banks=tr):
                dve.wait_ge(lhs_hi, b + 1)
                for j in range(2):
                    if gain is None:
                        h = hi[:, bass.ds(kb + 2 * j, 2), :].rearrange("p k s -> p (k s)").bitcast(F32)
                        dst = lo[:, bass.ds(kb + 2 * j, 2), :].rearrange("p k s -> p (k s)")
                        ins = nc.vector.tensor_tensor(dst, banks[j][:, :], h, ALU.subtract)
                    else:
                        for k in range(2):
                            kk = kb + 2 * j + k
                            ins = nc.vector.scalar_tensor_tensor(
                                out=lo[:, kk, :], in0=banks[j][:, k * S:(k + 1) * S],
                                scalar=gains[:, gain + kk:gain + kk + 1], in1=hi[:, kk, :].bitcast(F32),
                                op0=ALU.mult, op1=ALU.subtract)
                ins.then_inc(lhs_lo, 1)

            def add_residual(phase, n_hg, c, b, saved, in_place=False, done=None):
                dve.wait_ge(w_used, hg_before[phase] + (done or n_hg * (c + 1)))
                if not in_place:
                    dve.wait_ge(transposed, b)
                    if saved:
                        dve.wait_ge(res_saved, saved)
                for t in range(TT):
                    old = res[:, t, c * CH:(c + 1) * CH]
                    ins = nc.vector.tensor_tensor(old if in_place else stage[:, t, :], acc[c % 2][t][:, :], old,
                                                  ALU.add)
                ins.then_inc(staged, 1)

            def total_squares(n, saved):
                dve.wait_ge(res_saved, saved)
                nc.vector.tensor_reduce(rstd[:, n, :], sums[:, n, :, :], AX_X, ALU.add).then_inc(ms_ready, 1)

            dve.wait_ge(gains_ready, 1)
            def x_lo_part(c):
                lhs_lo_part(c, a_hi, a_lo, HPC * c, A_NORM, x_banks[c])

            def x_squares():
                dve.wait_ge(sums_ready, 1)
                nc.vector.tensor_copy(rstd[:, 0, :], sums[:, 0, :, 0]).then_inc(ms_ready, 1)

            def v_stats(c):
                dve.wait_ge(v_ready, c + 1)
                for t in range(TT):
                    step.inc(nc.vector.bn_stats(ln_stats[:, t, c, :], v_nat[:, t, c * CH:(c + 1) * CH]))
                if c == NC - 1:
                    step.wait()
                    for t in range(TT):
                        ins = nc.vector.bn_aggr(ln_mv[:, t, :], ln_stats[:, t, :, :].rearrange("p c s -> p (c s)"))
                    ins.then_inc(mv_ready, 1)

            def layer_norm(c):
                dve.wait_ge(ln_rstd_ready, 1)
                dve.wait_ge(ln_landed, 32)
                part = slice(c * CH, (c + 1) * CH)
                for t in range(TT):
                    step.inc(nc.vector.tensor_scalar(v_nat[:, t, part], v_nat[:, t, part], ln_mv[:, t, 0:1],
                                                     ln_rstd[:, t:t + 1], ALU.subtract, ALU.mult))
                step.wait()
                for t in range(TT):
                    step.inc(nc.vector.tensor_tensor(v_nat[:, t, part], v_nat[:, t, part], ln_gain[:, part], ALU.mult))
                step.wait()
                for t in range(TT):
                    ins = nc.vector.tensor_tensor(v_nat[:, t, part], v_nat[:, t, part], ln_bias[:, part], ALU.add)
                ins.then_inc(ln_done, 1)

            def gate(c):
                dve.wait_ge(mixed, c + 1)
                dve.wait_ge(u_ready, c + 1)
                dve.wait_ge(transposed, batches["gated"] + c)
                for t in range(TT):
                    for g in range(HPC):
                        cols = slice(g * P, (g + 1) * P)
                        col = B_S + HPC * c + g
                        ins = nc.vector.scalar_tensor_tensor(
                            out=stage[:, t, cols], in0=tr[t][:, cols], scalar=gains[:, col:col + 1],
                            in1=u_nat[:, t, cols], op0=ALU.add, op1=ALU.mult)
                ins.then_inc(staged, 1)

            x_lo_part(0)
            for c in range(NC):
                hooks = {5: [lambda c=c: v_stats(c - 1)]} if c else {
                    0: [lambda: x_lo_part(1)], 1: [lambda: x_lo_part(2)], 2: [lambda: x_lo_part(3)], 4: [x_squares]}
                unit(hg_before["v"] + 8 * c, hooks)
            for c in range(NC):
                if c == 0:
                    hooks = {5: [lambda: v_stats(NC - 1)], 7: [lambda: layer_norm(0)]}
                else:
                    hooks = {5: [lambda c=c: layer_norm(c)],
                             7: [lambda c=c: gate(c - 1),
                                 lambda c=c: lhs_lo_part(batches["gated"] + c - 1, g_hi, g_lo, HPC * (c - 1))]}
                unit(hg_before["u"] + 8 * c, hooks)
            for c in range(NC):
                if c == 0:
                    hooks = {7: [lambda: gate(NC - 1),
                                 lambda: lhs_lo_part(batches["gated"] + NC - 1, g_hi, g_lo, HPC * (NC - 1))]}
                else:
                    hooks = {3: [lambda c=c: add_residual("wout", 8, c - 1, batches["x1"] + c - 1, c - 1)],
                             7: [lambda c=c: lhs_lo_part(batches["x1"] + c - 1, a_hi, a_lo, HPC * (c - 1), FFN0)]}
                unit(hg_before["wout"] + 8 * c, hooks)

            def gate_up(layer, norm, first_hooks):
                base, b0 = hg_before[f"gu{layer}"], batches[f"h{layer}"]

                def hidden(i, u_end):
                    dve.wait_ge(w_used, u_end)
                    dve.wait_ge(silu_ready, i + (NF * layer + 1))
                    for t in range(TT):
                        ins = nc.vector.scalar_tensor_tensor(
                            out=stage[:, t, :], in0=acc[1][t][:, :], scalar=rstd[:, norm, t:t + 1],
                            in1=stage[:, t, :], op0=ALU.mult, op1=ALU.mult)
                    ins.then_inc(staged, 1)

                def body(i, first):
                    hooks = first_hooks if first else {
                        3: [lambda: hidden(i - 1, i * 16 + base)],
                        7: [lambda: lhs_lo_part(i + (b0 - 1), h_hi, h_lo, i * HPC - HPC)]}
                    unit(i * 16 + base, hooks)
                    unit(i * 16 + (base + 8), {})

                body(0, True)
                with dve.Fori(1, NF) as i:
                    body(i, False)
                return hidden

            def down(layer, hidden):
                base = hg_before[f"down{layer}"]
                n = FB // HG
                for c in range(NC):
                    if c == 0:
                        b = batches[f"h{layer}"] + NF - 1
                        hooks = {3: [lambda: hidden(NF - 1, base)],
                                 7: [lambda: lhs_lo_part(b, h_hi, h_lo, HPC * (NF - 1))]}
                    elif layer == 0:
                        hooks = {3: [lambda c=c: add_residual("down0", n, c - 1, batches["x2"] + c - 1, NC + c - 1)],
                                 7: [lambda c=c: lhs_lo_part(batches["x2"] + c - 1, a_hi, a_lo, HPC * (c - 1))]}
                    else:
                        hooks = {3: [lambda c=c: add_residual("down1", n, c - 1, 0, 0, in_place=True)]}
                    unit(base + n * c, hooks, j0=c % 2 * n, n=n)

            hidden = gate_up(0, 1, {
                3: [lambda: add_residual("wout", 8, NC - 1, batches["x1"] + NC - 1, NC - 1)],
                7: [lambda: total_squares(1, NC),
                    lambda: lhs_lo_part(batches["x1"] + NC - 1, a_hi, a_lo, HPC * (NC - 1), FFN0)]})
            down(0, hidden)

            base = hg_before["qkv"]
            last_x2 = batches["x2"] + NC - 1

            def square_sums(i, n):
                dve.wait_ge(kq_squared, i * 2 + (n + 1))
                nc.vector.tensor_reduce(head_ss[:, n, :, :], sq_nat[:, :, :, :], AX_X, ALU.add).then_inc(kq_ss, 1)

            def norm_heads(i, n):
                dve.wait_ge(kq_rs, i * 2 + (n + 1))
                nat = (k_nat, q_nat)[n][:, :, :, :].rearrange("p t h d -> p (t h) d")
                rs = head_rs[:, n, :, :].rearrange("p t (h a) -> p (t h) a", a=1).to_broadcast([P, TT * HPC, P])
                nc.vector.tensor_tensor(nat, nat, rs, ALU.mult).then_inc(kq_normed, 1)

            def maxima(i, h):
                dve.wait_ge(scored, i * HPC + (h + 1))
                step.inc(nc.vector.tensor_tensor(score[:, :, :].rearrange("p n s -> p (n s)"), tr[0][:, 0:3 * P],
                                                 mask[:, :, :].rearrange("p n s -> p (n s)"), ALU.add))
                step.wait()
                for t, (a, b) in enumerate(((0, 1), (1, 3))):
                    ins = nc.vector.tensor_reduce(neg_max[:, t:t + 1], score[:, a:b, :].rearrange("p n s -> p (n s)"),
                                                  AX_X, ALU.max, negate=True)
                ins.then_inc(maxed, 1)

            def head_output(i, h):
                dve.wait_ge(exped, i * HPC + (h + 1))
                step.inc(nc.vector.reciprocal(row_inv[:, :], row_sum[:, :]))
                step.wait()
                dve.wait_ge(pv_done, i * HPC + (h + 1))
                if h == 0:
                    dve.wait_ge(transposed, i + batches["o"])
                    dve.wait_ge(res_saved, 2 * NC)
                for t in range(TT):
                    ins = nc.vector.tensor_scalar(stage[:, t, h * P:(h + 1) * P], tr[1][:, t * P:(t + 1) * P],
                                                  row_inv[:, t:t + 1], None, ALU.mult)
                ins.then_inc(staged if h == HPC - 1 else head_out, 1)

            def o_lo_part(i):
                lhs_lo_part(i + batches["o"], o_hi, o_lo, i * HPC)

            def attention_hooks(i):
                hooks = {4: [lambda: square_sums(i, 1)], 6: [lambda: norm_heads(i, 1)], 11: [lambda: maxima(i, 0)]}
                for h in range(HPC):
                    hooks[14 + 3 * h] = [lambda h=h: head_output(i, h)]
                    if h < HPC - 1:
                        hooks[14 + 3 * h].append(lambda h=h: maxima(i, h + 1))
                hooks[23].append(lambda: o_lo_part(i))
                return hooks

            def qkv_body(i, first):
                if first:
                    hooks = {3: [lambda: add_residual("down0", FB // HG, NC - 1, last_x2, 2 * NC - 1)],
                             7: [lambda: total_squares(2, 2 * NC),
                                 lambda: lhs_lo_part(last_x2, a_hi, a_lo, HPC * (NC - 1))]}
                else:
                    hooks = attention_hooks(i - 1)
                hooks[20] = hooks.get(20, []) + [lambda: square_sums(i, 0)]
                hooks[22] = [lambda: norm_heads(i, 0)]
                for n, gain in enumerate((KV_NORM, KV_NORM, B_NORM)):
                    unit(i * 24 + (base + 8 * n),
                         {j - 8 * n: f for j, f in hooks.items() if 8 * n <= j < 8 * n + 8}, gain=gain)

            qkv_body(0, True)
            dve.wait_ge(mask_ready, 2)
            with dve.Fori(1, NC) as i:
                step.enter(i, 2 * HPC, first=1)
                qkv_body(i, False)
                step.leave(NC)

            g = NC - 1
            hooks = {3: [lambda: square_sums(g, 1)], 4: [lambda: norm_heads(g, 1)]}
            for h in range(HPC):
                hooks.setdefault(6 + 2 * h, []).append(lambda h=h: maxima(g, h))
                hooks[8 + 2 * h] = [lambda h=h: head_output(g, h)]
            hooks[14].append(lambda: o_lo_part(g))
            unit(hg_before["wo"], hooks, n=16)

            def x3(c):
                done = 14 if c == 0 else None
                return [lambda: add_residual("wo", 8, c, batches["x3"] + c, 2 * NC + c, done=done)]

            def x3_lo(c):
                return [lambda: lhs_lo_part(batches["x3"] + c, a_hi, a_lo, HPC * c, FFN1)]

            unit(hg_before["wo"] + 16, {1: x3(0), 7: x3_lo(0) + x3(1)})
            unit(hg_before["wo"] + 24, {3: x3_lo(1) + x3(2), 7: x3_lo(2)})
            hidden = gate_up(1, 3, {
                3: [lambda: add_residual("wo", 8, NC - 1, batches["x3"] + NC - 1, 3 * NC - 1)],
                7: [lambda: total_squares(3, 3 * NC),
                    lambda: lhs_lo_part(batches["x3"] + NC - 1, a_hi, a_lo, HPC * (NC - 1), FFN1)]})
            down(1, hidden)
            add_residual("down1", FB // HG, NC - 1, 0, 0, in_place=True)

        @block.tensor
        def _(pe):
            def half_group(m, hi, lo, s, j, slot, n):
                pe.wait_ge(lo_split, m + 1)
                for k in range(HG):
                    kb = HG * j + k
                    for t in range(TT):
                        tok = slice(t * P, (t + 1) * P)
                        nc.tensor.matmul(acc[s][t][:, :], hi[:, kb, tok], w_hi[:, slot, k, :],
                                         start=kb == 0, stop=False)
                        nc.tensor.matmul(acc[s][t][:, :], hi[:, kb, tok], w_lo[:, slot, k, :],
                                         start=False, stop=False)
                        ins = nc.tensor.matmul(acc[s][t][:, :], lo[:, kb, tok], w_hi[:, slot, k, :],
                                               start=False, stop=kb == HG * n - 1)
                ins.then_inc(w_used, 1)

            def unit(m0, hi, lo, s, hooks={}, lhs_waits={}, j0=0, n=KB // HG):
                for j in range(n):
                    if j in lhs_waits:
                        pe.wait_ge(lhs_lo, lhs_waits[j])
                    half_group(m0 + j, hi, lo, s, j, (j0 + j) % RING, n)
                    for work in hooks.get(j, ()):
                        work()

            def transpose_batch(b, src=None, banks=tr):
                if src is None:
                    pe.wait_ge(staged, b + 1 - NC)
                    pe.wait_ge(lhs_lo, b)
                for j in range(2):
                    for k in range(2):
                        for t in range(TT):
                            blk = slice((2 * j + k) * P, (2 * j + k + 1) * P)
                            from_ = stage[:, t, blk] if src is None else src[:, t, blk]
                            ins = nc.tensor.transpose(banks[j][:, k * S + t * P:k * S + (t + 1) * P], from_, ident[:, :])
                ins.then_inc(transposed, 1)

            pe.wait_ge(ident_ready, 1)
            pe.wait_ge(rows_landed, 6 * 16)
            nc.tensor.transpose(acc[0][0][:, 0:6 * KB], rows[:, :], ident[0:6 * KB, 0:6 * KB]).then_inc(rows_transposed, 1)

            def transpose_x(c):
                pe.wait_ge(x_landed[c], 16)
                if c == NC - 1:
                    pe.wait_ge(lhs_lo, 1)
                transpose_batch(c, res[:, :, c * CH:(c + 1) * CH], x_banks[c])

            for c in range(NC - 1):
                transpose_x(c)

            pe.wait_ge(gains_ready, 1)
            unit(hg_before["v"], a_hi, a_lo, 0,
                 {0: [lambda: transpose_x(NC - 1)]},
                 {0: 1, 2: 2, 4: 3, 6: 4})
            unit(hg_before["v"] + 8, a_hi, a_lo, 1)
            with pe.Fori(1, NC // 2) as i:
                for s in range(2):
                    pe.wait_ge(v_ready, i * 2 + (s - 1))
                    unit(i * 16 + (hg_before["v"] + 8 * s), a_hi, a_lo, s)

            pe.wait_ge(ws_masked, 1)
            for n, bank in enumerate((tr[0], tr[1], acc[2][0], acc[2][1])):
                for g in range(4):
                    ins = nc.tensor.transpose(bank[:, g * P:(g + 1) * P], w_s_nat[:, 4 * n + g, :], ident[:, :])
            ins.then_inc(wsT_done, 1)

            def mix(c):
                pe.wait_ge(ln_done, c + 1)
                if c == 0:
                    pe.wait_ge(wsT_ready, 1)
                pe.wait_ge(lhs_lo, batches["gated"] + c)
                for t in range(TT):
                    for g in range(HPC):
                        gg = HPC * c + g
                        ins = nc.tensor.matmul(tr[t][:, g * P:(g + 1) * P], w_sT[:, gg, :],
                                               v_nat[:, t, gg * P:(gg + 1) * P], start=True, stop=True)
                ins.then_inc(mixed, 1)

            def gated_hooks(c):
                return {3: [lambda: mix(c)], 4 if c == NC - 1 else 5: [lambda: transpose_batch(batches["gated"] + c)]}

            for c in range(NC):
                if c < 2:
                    pe.wait_ge(v_ready, NC - 1 + c)
                else:
                    pe.wait_ge(u_ready, c - 1)
                unit(hg_before["u"] + 8 * c, a_hi, a_lo, c % 2, gated_hooks(c - 1) if c else {})

            last = batches["gated"] + NC - 1
            pe.wait_ge(u_ready, NC - 1)
            unit(hg_before["wout"], g_hi, g_lo, 0, gated_hooks(NC - 1), {0: last, 6: last + 1})
            pe.wait_ge(u_ready, NC)
            unit(hg_before["wout"] + 8, g_hi, g_lo, 1, {3: [lambda: transpose_batch(batches["x1"])]})
            with pe.Fori(1, NC // 2) as i:
                for s in range(2):
                    pe.wait_ge(staged, i * 2 + (batches["x1"] - NC + s - 1))
                    unit(i * 16 + (hg_before["wout"] + 8 * s), g_hi, g_lo, s,
                         {3: [lambda s=s: transpose_batch(i * 2 + (batches["x1"] + s - 1))]})

            def gate_up(layer):
                base, b0 = hg_before[f"gu{layer}"], batches[f"h{layer}"]
                with pe.Fori(0, NF) as i:
                    pe.wait_ge(staged, i + (b0 - 1 - NC))
                    unit(i * 16 + base, a_hi, a_lo, 0, {3: [lambda: transpose_batch(i + (b0 - 1))]}, {0: b0 - 1, 6: b0})
                    pe.wait_ge(staged, i + (b0 - NC))
                    unit(i * 16 + (base + 8), a_hi, a_lo, 1)
                    pe.wait_ge(silu_ready, i + (NF * layer + 1))

            def down(layer):
                base, n = hg_before[f"down{layer}"], FB // HG
                b0 = batches["x2" if layer == 0 else "out"]
                unit(base, h_hi, h_lo, 0, {3: [lambda: transpose_batch(b0 - 1)]}, {0: b0 - 1, n - 2: b0}, n=n)
                pe.wait_ge(staged, b0 - NC)
                unit(base + n, h_hi, h_lo, 1, {3: [lambda: transpose_batch(b0)]} if layer == 0 else {}, j0=n, n=n)
                with pe.Fori(1, NC // 2) as i:
                    for s in range(2):
                        pe.wait_ge(staged, i * 2 + (b0 - NC + s - 1))
                        unit(i * 2 * n + (base + n * s), h_hi, h_lo, s,
                             {3: [lambda s=s: transpose_batch(i * 2 + (b0 + s - 1))]} if layer == 0 else {},
                             j0=n * s, n=n)

            gate_up(0)
            down(0)

            def transpose_heads(i, n):
                pe.wait_ge(kq_normed, i * 2 + (n + 1))
                if n == 0:
                    pe.wait_ge(lhs_lo, i + batches["o"])
                else:
                    pe.wait_ge(kq_ready, i * 2 + 1)
                nat = (k_nat, q_nat)[n]
                for h in range(HPC):
                    for t in range(TT):
                        at = h % 2 * S + t * P
                        ins = nc.tensor.transpose(tr[h // 2][:, at:at + P], nat[:, t, h, :], ident[:, :])
                ins.then_inc(kq_transposed, 1)

            def scores(i, h):
                if h == 0:
                    pe.wait_ge(kq_ready, i * 2 + 2)
                else:
                    pe.wait_ge(maxed, i * HPC + h)
                nc.tensor.matmul(tr[0][:, 0:P], qT[:, h, 0:P], kT[:, h, 0:P], start=True, stop=True)
                nc.tensor.matmul(tr[0][:, P:3 * P], qT[:, h, P:2 * P], kT[:, h, 0:2 * P],
                                 start=True, stop=True).then_inc(scored, 1)

            def transpose_probs(i, h):
                pe.wait_ge(exped, i * HPC + (h + 1))
                if h:
                    pe.wait_ge(head_out, i * (HPC - 1) + h)
                for n in range(3):
                    ins = nc.tensor.transpose(tr[1][:, n * P:(n + 1) * P], prob[:, n, :], ident[:, :])
                ins.then_inc(probT_done, 1)

            def values(i, h):
                pe.wait_ge(probT_ready, i * HPC + (h + 1))
                if h == 0:
                    pe.wait_ge(val_ready, i + 1)
                v = [val[:, t, bass.ds(i * CH + h * P, P)] for t in range(TT)]
                nc.tensor.matmul(tr[1][:, 0:P], probT[:, 0, :], v[0], start=True, stop=True)
                nc.tensor.matmul(tr[1][:, P:2 * P], probT[:, 1, :], v[0], start=True, stop=False)
                nc.tensor.matmul(tr[1][:, P:2 * P], probT[:, 2, :], v[1], start=False, stop=True).then_inc(pv_done, 1)

            def attention_hooks(i):
                hooks = {3: [lambda: transpose_heads(i, 0)], 5: [lambda: transpose_heads(i, 1)]}
                for h in range(HPC):
                    hooks.setdefault(7 + 3 * h, []).append(lambda h=h: scores(i, h))
                    hooks[9 + 3 * h] = [lambda h=h: transpose_probs(i, h)]
                    hooks[10 + 3 * h] = [lambda h=h: values(i, h)]
                hooks[21] = [lambda: transpose_batch(i + batches["o"])]
                return hooks

            base = hg_before["qkv"]

            def qkv_body(i, hooks, lhs_waits):
                for n in range(3):
                    if not isinstance(i, int):
                        if n == 0:
                            pe.wait_ge(val_ready, i)
                        else:
                            pe.wait_ge(kq_raw, i * 2 + (n - 2))
                    elif n < 2:
                        pe.wait_ge(staged, batches["x2"] + 3 + n - NC)
                    unit(i * 24 + (base + 8 * n), a_hi, a_lo, n,
                         {j - 8 * n: f for j, f in hooks.items() if 8 * n <= j < 8 * n + 8}, lhs_waits if n == 0 else {})

            b_last = batches["x2"] + NC - 1
            qkv_body(0, {3: [lambda: transpose_batch(b_last)]}, {0: b_last, 6: b_last + 1})
            with pe.Fori(1, NC) as i:
                qkv_body(i, attention_hooks(i - 1), {})

            g = NC - 1
            hooks = {1: [lambda: transpose_heads(g, 0)], 2: [lambda: transpose_heads(g, 1)]}
            for h in range(HPC):
                hooks.setdefault(3 + 2 * h, []).append(lambda h=h: scores(g, h))
                hooks[4 + 2 * h] = [lambda h=h: transpose_probs(g, h)]
                hooks.setdefault(5 + 2 * h, []).insert(0, lambda h=h: values(g, h))
            hooks[11].append(lambda: transpose_batch(batches["o"] + g))
            pe.wait_ge(lhs_lo, batches["o"] + g)
            pe.wait_ge(val_ready, NC)
            pe.wait_ge(kq_raw, 2 * NC - 1)
            for n, (c, kg) in enumerate(WO_FIRST):
                if kg == 3 and c == 0:
                    pe.wait_ge(lhs_lo, batches["o"] + NC)
                for j in range(2):
                    half_group(hg_before["wo"] + 2 * n + j, o_hi, o_lo, c, 2 * kg + j, (2 * n + j) % RING, KB // HG)
                    for work in hooks.get(2 * n + j, ()):
                        work()

            def x3(c):
                return [lambda: transpose_batch(batches["x3"] + c)]

            pe.wait_ge(staged, batches["x3"] - NC + 1)
            unit(hg_before["wo"] + 16, o_hi, o_lo, 0, {3: x3(0), 7: x3(1)})
            pe.wait_ge(staged, batches["x3"] - NC + 2)
            unit(hg_before["wo"] + 24, o_hi, o_lo, 1, {3: x3(2)})
            gate_up(1)
            down(1)


_INS = ["x", "a_norm", "a_w_in", "a_ln_g", "a_ln_b", "a_w_s", "a_b_s", "a_w_out", "kv_norm", "w_k", "w_v", "k_norm",
        "b_norm", "b_w_q", "b_q_norm", "b_w_o", "ffn_norm", "ffn_w_gate", "ffn_w_up", "ffn_w_down"]


def kernel(**inputs):
    import numpy as _np
    import concourse.bacc as _bacc
    from concourse import mybir as _mybir
    from concourse.bass_utils import run_bass_kernel_spmd as _run

    nc = _bacc.Bacc("TRN2", target_bir_lowering=False, num_devices=1)
    arrays, args = {}, []
    for name in _INS:
        a = _np.ascontiguousarray(inputs[name])
        arrays[f"in_{name}_dram"] = a
        args.append(nc.dram_tensor(f"in_{name}_dram", a.shape, _mybir.dt.from_np(a.dtype), kind="ExternalInput").ap())
    shape = tuple(inputs["x"].shape)
    args.append(nc.dram_tensor("out_0_dram", shape, _mybir.dt.float32, kind="ExternalOutput").ap())
    yoco_kernel(nc, *args)
    r = _run(nc, [arrays], core_ids=[0])
    return r.results[0]["out_0_dram"]
```
